# Optimizing a Trainium2 kernel written in Bass

```python
import math
import jax, jax.numpy as jnp
from jax import lax
import numpy as np

D_MODEL = 1024
BATCH = 1
SEQ = 512
DEPTH = 1

HEAD_DIM = 64
ATTN_WIDTH = D_MODEL // 2
ATTN_HEADS = ATTN_WIDTH // HEAD_DIM
MOBA_BLOCK = 256
MOBA_TOPK = 3
Q_CHUNK = 64
POOL_WIDTH = D_MODEL // 4
POOL_WINDOWS = (2, 4, 8, 16)
POOL_GROUPS = len(POOL_WINDOWS)
POOL_GROUP_DIM = POOL_WIDTH // POOL_GROUPS
CONV_WIDTH = D_MODEL // 4
CONV_KERNEL = 31
N_BRANCHES = 3
D_FF = -(-8 * D_MODEL // (3 * 256)) * 256
REL_BUCKETS = 32
REL_MAX_DIST = 128
EPS = 1e-6
NEG = -1e30
IN_WIDTH = 3 * ATTN_WIDTH + POOL_WIDTH + 2 * CONV_WIDTH + N_BRANCHES * D_MODEL
IN_SPLITS = [ATTN_WIDTH, 2 * ATTN_WIDTH, 3 * ATTN_WIDTH,
             3 * ATTN_WIDTH + POOL_WIDTH,
             3 * ATTN_WIDTH + POOL_WIDTH + 2 * CONV_WIDTH]

kernel_name = "hybrid_gated_moba_pool_conv_block"

def rms_norm(x, g):
    xf = x.astype(jnp.float32)
    y = xf * lax.rsqrt(jnp.mean(xf * xf, axis=-1, keepdims=True) + EPS)
    return (y * g.astype(jnp.float32)).astype(x.dtype)

def t5_bucket(rel):
    n = jnp.maximum(rel, 0)
    max_exact = REL_BUCKETS // 2
    nf = jnp.maximum(n, 1).astype(jnp.float32)
    large = max_exact + (jnp.log(nf / max_exact) / math.log(REL_MAX_DIST / max_exact)
                         * (REL_BUCKETS - max_exact)).astype(jnp.int32)
    large = jnp.minimum(large, REL_BUCKETS - 1)
    return jnp.where(n < max_exact, n, large)

def moba_attention(q, k, v, rel_bias):
    B, H, S, dh = q.shape
    n_blocks = -(-S // MOBA_BLOCK)
    s_pad = n_blocks * MOBA_BLOCK
    pad = ((0, 0), (0, 0), (0, s_pad - S), (0, 0))
    q, k, v = jnp.pad(q, pad), jnp.pad(k, pad), jnp.pad(v, pad)
    k_blocks = k.reshape(B, H, n_blocks, MOBA_BLOCK, dh)
    v_blocks = v.reshape(B, H, n_blocks, MOBA_BLOCK, dh)
    k_mean = jnp.mean(k_blocks.astype(jnp.float32), axis=3)
    n_sel = min(MOBA_TOPK, n_blocks)
    scale = HEAD_DIM ** -0.5
    table_t = rel_bias.T.astype(jnp.float32)
    b_ix = jnp.arange(B)[:, None, None, None]
    h_ix = jnp.arange(H)[None, :, None, None]
    offs = jnp.arange(MOBA_BLOCK)
    blk_ids = jnp.arange(n_blocks)

    def chunk(start):
        blk = start // MOBA_BLOCK
        qf = lax.dynamic_slice_in_dim(q, start, Q_CHUNK, axis=2).astype(jnp.float32)
        q_pos = start + jnp.arange(Q_CHUNK)
        gate = jnp.einsum('bhqd,bhnd->bhqn', qf, k_mean)
        gate = jnp.where(blk_ids < blk, gate, -jnp.inf)
        _, idx = lax.top_k(gate, n_sel)
        sel_ok = idx < blk
        k_sel = k_blocks[b_ix, h_ix, idx].astype(jnp.float32)
        v_sel = v_blocks[b_ix, h_ix, idx].astype(jnp.float32)
        k_pos_sel = idx[..., None] * MOBA_BLOCK + offs
        bias_sel = table_t[h_ix[..., None], t5_bucket(q_pos[:, None, None] - k_pos_sel)]
        logit_sel = jnp.einsum('bhqd,bhqjkd->bhqjk', qf, k_sel) * scale + bias_sel
        logit_sel = jnp.where(sel_ok[..., None], logit_sel, NEG)
        own_start = blk * MOBA_BLOCK
        k_own = lax.dynamic_slice_in_dim(k, own_start, MOBA_BLOCK, axis=2).astype(jnp.float32)
        v_own = lax.dynamic_slice_in_dim(v, own_start, MOBA_BLOCK, axis=2).astype(jnp.float32)
        rel_own = q_pos[:, None] - (own_start + offs)[None, :]
        bias_own = table_t[:, t5_bucket(rel_own)]
        logit_own = jnp.einsum('bhqd,bhkd->bhqk', qf, k_own) * scale + bias_own
        logit_own = jnp.where(rel_own >= 0, logit_own, NEG)
        logits = jnp.concatenate(
            [logit_sel.reshape(B, H, Q_CHUNK, n_sel * MOBA_BLOCK), logit_own], axis=-1)
        probs = jax.nn.softmax(logits, axis=-1)
        p_sel = probs[..., :n_sel * MOBA_BLOCK].reshape(B, H, Q_CHUNK, n_sel, MOBA_BLOCK)
        p_own = probs[..., n_sel * MOBA_BLOCK:]
        out = (jnp.einsum('bhqjk,bhqjkd->bhqd', p_sel, v_sel)
               + jnp.einsum('bhqk,bhkd->bhqd', p_own, v_own))
        return out.astype(q.dtype)

    starts = jnp.arange(0, s_pad, Q_CHUNK, dtype=jnp.int32)
    outs = lax.map(chunk, starts)
    out = outs.transpose(1, 2, 0, 3, 4).reshape(B, H, s_pad, dh)
    return out[:, :, :S]

def pool_mixer(u, w_group, scale):
    B, S, C = u.shape
    uf = u.astype(jnp.float32)
    cs = jnp.cumsum(uf, axis=1)
    t = jnp.arange(1, S + 1, dtype=jnp.float32)[:, None]
    parts = []
    for g, w in enumerate(POOL_WINDOWS):
        sl = slice(g * POOL_GROUP_DIM, (g + 1) * POOL_GROUP_DIM)
        c = cs[..., sl]
        lag = jnp.pad(c, ((0, 0), (w, 0), (0, 0)))[:, :S]
        parts.append((c - lag) / jnp.minimum(t, float(w)) - uf[..., sl])
    d = jnp.stack(parts, axis=2)
    y = jnp.einsum('bsgc,gcd->bsgd', d, w_group.astype(jnp.float32)).reshape(B, S, C)
    return (y * scale.astype(jnp.float32)).astype(u.dtype)

def conv_module(u_glu, w_dw, b_dw, ln_g, ln_b):
    a, gt = jnp.split(u_glu, 2, axis=-1)
    u = a * jax.nn.sigmoid(gt)
    y = lax.conv_general_dilated(
        u, w_dw[:, None, :].astype(u.dtype), window_strides=(1,),
        padding=[(CONV_KERNEL - 1, 0)], dimension_numbers=('NWC', 'WIO', 'NWC'),
        feature_group_count=CONV_WIDTH) + b_dw
    yf = y.astype(jnp.float32)
    mu = jnp.mean(yf, axis=-1, keepdims=True)
    var = jnp.mean(jnp.square(yf - mu), axis=-1, keepdims=True)
    yn = (yf - mu) * lax.rsqrt(var + EPS) * ln_g + ln_b
    return jax.nn.silu(yn).astype(u.dtype)

def setup_inputs(seed: int = 0) -> dict:
    key = jax.random.key(seed)
    ks = jax.random.split(key, 20)

    def nrm(k, shape, s):
        return jax.random.normal(k, shape, jnp.float32) * s

    gd = POOL_GROUP_DIM
    return {
        "x": nrm(ks[0], (BATCH, SEQ, D_MODEL), 1.0),
        "pre_mix_g": 1.0 + nrm(ks[1], (DEPTH, D_MODEL), 0.1),
        "w_in": nrm(ks[2], (DEPTH, D_MODEL, IN_WIDTH), D_MODEL ** -0.5),
        "b_gate": nrm(ks[3], (DEPTH, N_BRANCHES * D_MODEL), 0.1),
        "w_attn_o": nrm(ks[4], (DEPTH, ATTN_WIDTH, D_MODEL), ATTN_WIDTH ** -0.5),
        "rel_bias": nrm(ks[5], (REL_BUCKETS, ATTN_HEADS), 0.5),
        "w_pool_g": nrm(ks[6], (DEPTH, POOL_GROUPS, gd, gd), gd ** -0.5),
        "pool_scale": 1.0 + nrm(ks[7], (DEPTH, POOL_WIDTH), 0.1),
        "w_pool_o": nrm(ks[8], (DEPTH, POOL_WIDTH, D_MODEL), POOL_WIDTH ** -0.5),
        "w_dw": nrm(ks[9], (DEPTH, CONV_KERNEL, CONV_WIDTH), CONV_KERNEL ** -0.5),
        "b_dw": nrm(ks[10], (DEPTH, CONV_WIDTH), 0.02),
        "conv_ln_g": 1.0 + nrm(ks[11], (DEPTH, CONV_WIDTH), 0.1),
        "conv_ln_b": nrm(ks[12], (DEPTH, CONV_WIDTH), 0.02),
        "w_conv_o": nrm(ks[13], (DEPTH, CONV_WIDTH, D_MODEL), CONV_WIDTH ** -0.5),
        "w_out": nrm(ks[14], (DEPTH, D_MODEL, D_MODEL), D_MODEL ** -0.5),
        "post_mix_g": 1.0 + nrm(ks[15], (DEPTH, D_MODEL), 0.1),
        "pre_ffn_g": 1.0 + nrm(ks[16], (DEPTH, D_MODEL), 0.1),
        "w_ffn_in": nrm(ks[17], (DEPTH, D_MODEL, 2 * D_FF), D_MODEL ** -0.5),
        "w_ffn_out": nrm(ks[18], (DEPTH, D_FF, D_MODEL), D_FF ** -0.5),
        "post_ffn_g": 1.0 + nrm(ks[19], (DEPTH, D_MODEL), 0.1),
    }

def reference(x, pre_mix_g, w_in, b_gate, w_attn_o, rel_bias, w_pool_g, pool_scale,
              w_pool_o, w_dw, b_dw, conv_ln_g, conv_ln_b, w_conv_o, w_out, post_mix_g,
              pre_ffn_g, w_ffn_in, w_ffn_out, post_ffn_g):
    B, S, D = x.shape
    for l in range(DEPTH):
        h = rms_norm(x, pre_mix_g[l])
        proj = h @ w_in[l]
        q, k, v, u_pool, u_conv, g_logits = jnp.split(proj, IN_SPLITS, axis=-1)

        def heads(t):
            return t.reshape(B, S, ATTN_HEADS, HEAD_DIM).transpose(0, 2, 1, 3)

        attn = moba_attention(heads(q), heads(k), heads(v), rel_bias)
        attn = attn.transpose(0, 2, 1, 3).reshape(B, S, ATTN_WIDTH) @ w_attn_o[l]
        pool = pool_mixer(u_pool, w_pool_g[l], pool_scale[l]) @ w_pool_o[l]
        conv = conv_module(u_conv, w_dw[l], b_dw[l], conv_ln_g[l], conv_ln_b[l]) @ w_conv_o[l]
        gates = jax.nn.sigmoid(g_logits + b_gate[l]).reshape(B, S, N_BRANCHES, D)
        merged = gates[:, :, 0] * attn + gates[:, :, 1] * pool + gates[:, :, 2] * conv
        x = x + rms_norm(merged @ w_out[l], post_mix_g[l])
        h = rms_norm(x, pre_ffn_g[l])
        gt, up = jnp.split(h @ w_ffn_in[l], 2, axis=-1)
        f = (jax.nn.silu(gt) * up) @ w_ffn_out[l]
        x = x + rms_norm(f, post_ffn_g[l])
    return x


_drawn_inputs = setup_inputs


def setup_inputs(seed=0):
    import zlib

    import numpy as np

    out = dict(_drawn_inputs(seed))
    spreads = {}
    factors = {'b_dw': 2.787, 'conv_ln_b': 6.365}
    for name, (base, spread) in spreads.items():
        noise = np.random.default_rng([zlib.crc32(name.encode()), seed]).standard_normal(out[name].shape)
        drawn = base * np.exp(spread * noise) if base else spread * noise
        out[name] = __import__('jax').numpy.asarray(drawn.astype(out[name].dtype))
    for name, factor in factors.items():
        out[name] = (out[name] * factor).astype(out[name].dtype)
    return out
```

```python
import math
from contextlib import ExitStack

import numpy as np

import concourse.bass as bass
from concourse import mybir

F32 = mybir.dt.float32
F32R = mybir.dt.float32r
BF16 = mybir.dt.bfloat16
ALU = mybir.AluOpType
ACT = mybir.ActivationFunctionType

P = 128
SEQ = 512
D_MODEL = 1024
DFF = 2816
TOK = SEQ // P
KT = D_MODEL // P
PAIRS = 4
HEAD = 64
ATT = 512
GATES = 3 * KT
COL_Q, COL_K, COL_V, COL_POOL = 0, ATT, 2 * ATT, 3 * ATT
COL_CONV = COL_POOL + 256
COL_GATE = COL_CONV + 512
CONV_K = 31
CONV_PAD = 32
POOL_PAD = 16
EPS = 1e-6
BIAS_LEN = 640
MASKED = -1e30

FIRST_UNITS = 6
PAIR_UNITS = 9
U_MIX = FIRST_UNITS + PAIRS * PAIR_UNITS
U_OUT = U_MIX + KT
U_FF = U_OUT + 8
FF_TILES = DFF // P
U_DOWN = U_FF + 2 * FF_TILES
U_END = U_DOWN + FF_TILES
RING = 3

V_PRE, V_GATE, V_PSCALE, V_BDW, V_LNG, V_LNB, V_DW = 0, 8, 32, 34, 36, 38, 40
V_LEN = 40 + 2 * CONV_K
C_RATIO, C_INV = 0, 32
C_LEN = 34


def in_ring(u):
    return u if u < U_OUT else u - 8


def build(nc, x, w_in, w_branch, w_out, w_ffn_in, w_ffn_out, vecs, post_mix_g, pre_ffn_g, post_ffn_g,
          rel_bias, w_pool_g, onehot, pool_const, out):
    bias_scratch = nc.dram_tensor("bias_scratch", (2 * PAIRS, BIAS_LEN), F32, kind="Internal").ap()

    base = 16512

    def at(name, kb, shape, dtype=F32):
        return nc.alloc_sbuf_tensor_at(name, [P] + shape, dtype, offset=base + int(kb * 1024))

    raw = at("raw", 0, [RING, 1024])
    w_hi = at("w_hi", 12, [RING, 1024], F32R)
    w_lo = at("w_lo", 24, [RING, 1024], F32R)
    h_hi = at("h_hi", 36, [KT, SEQ], F32R)
    h_lo = at("h_lo", 52, [KT, SEQ], F32R)
    gate = at("gate", 68, [GATES, SEQ])
    br_hi = at("br_hi", 116, [KT, SEQ], F32R)
    br_lo = at("br_lo", 132, [KT, SEQ], F32R)
    onehot_sb = at("onehot_sb", 68, [BIAS_LEN])
    table = at("table", 71, [8])
    bias_vec = at("bias_vec", 72, [BIAS_LEN])
    junk_x = at("junk_x", 76, [D_MODEL], BF16)
    conv_gate = at("conv_gate", 96, [2, SEQ])
    u_pool = at("u_pool", 190, [2, POOL_PAD + SEQ])
    sum_a = at("sum_a", 194.25, [2, POOL_PAD + SEQ])
    sum_b = at("sum_b", 109, [2, POOL_PAD + SEQ])
    u_conv = at("u_conv", 124, [2, CONV_PAD + SEQ])
    d_pool = at("d_pool", 140, [2, SEQ])
    conv_acc = at("conv_acc", 144, [2, SEQ])
    x_tok = at("x_tok", 162, [TOK, D_MODEL])
    qT_hi = at("qT_hi", 148, [SEQ], F32R)
    qT_lo = at("qT_lo", 150, [SEQ], F32R)
    kT_hi = at("kT_hi", 152, [SEQ], F32R)
    kT_lo = at("kT_lo", 154, [SEQ], F32R)
    vT = at("vT", 156, [SEQ])
    v_hi = at("v_hi", 158, [SEQ], F32R)
    v_lo = at("v_lo", 160, [SEQ], F32R)
    pT_hi = at("pT_hi", 162, [TOK, SEQ], F32R)
    pT_lo = at("pT_lo", 170, [TOK, SEQ], F32R)
    neg_logit = at("neg_logit", 178, [2, SEQ])
    prob = at("prob", 182, [2, SEQ])
    bias_h = at("bias_h", 186, [2, SEQ])
    t1 = at("t1", 190, [2, SEQ], F32R)
    t2 = at("t2", 194, [2, SEQ], F32R)
    t3 = at("t3", 198, [2, SEQ])
    mix = at("mix", 190, [2, 3, SEQ])
    wo_hi = [at("wo0_hi", 148, [KT, SEQ], F32R), at("wo1_hi", 68, [KT, SEQ], F32R)]
    wo_lo = [at("wo0_lo", 164, [KT, SEQ], F32R), at("wo1_lo", 84, [KT, SEQ], F32R)]
    x1 = at("x1", 180, [TOK, D_MODEL])
    gain = at("gain", 196, [D_MODEL])
    junk = at("junk", 200, [D_MODEL], BF16)
    xn = at("xn", 100, [2, D_MODEL])
    y_gain = at("y_gain", 108, [D_MODEL])
    gain_ffn = at("gain_ffn", 112, [D_MODEL])
    f_hi = at("f_hi", 68, [FF_TILES, SEQ], F32R)
    f_lo = at("f_lo", 112, [FF_TILES, SEQ], F32R)
    ff_tanh = at("ff_tanh", 156, [2, SEQ])
    ff_silu = at("ff_silu", 160, [2, SEQ])
    ff_prod = at("ff_prod", 164, [2, SEQ])
    yg0 = at("yg0", 36, [TOK, SEQ])
    yg1 = at("yg1", 44, [2, SEQ])
    ident = at("ident", 202, [P])
    mean_w = at("mean_w", 202.5, [P], F32R)
    pool_w = at("pool_w", 203, [2, P])
    pool_w_hi = at("pool_w_hi", 204, [2, P], F32R)
    pool_w_lo = at("pool_w_lo", 205, [2, P], F32R)
    vec = at("vec", 206, [V_LEN])
    const = at("const", 206.5, [C_LEN])
    half_bias = at("half_bias", 206.75, [GATES])
    half_dw = at("half_dw", 207, [2 * CONV_K])
    neg_max = at("neg_max", 207.25, [8])
    row_sum = at("row_sum", 207.28125, [8])
    row_inv = at("row_inv", 207.3125, [8])
    stat = at("stat", 207.34375, [96])
    spare = at("spare", 207.75, [8])

    with ExitStack() as ctx:
        bank = [ctx.enter_context(nc.psum_tensor(f"bank{i}", [P, SEQ], F32)) for i in range(8)]

        def sem(name):
            return ctx.enter_context(nc.semaphore(name))

        raw_full = [sem(f"raw_full{i}") for i in range(RING)]
        x_full = [sem(f"x_full{i}") for i in range(TOK)]
        x1_full, gain_full, vec_full, tab_full, pool_w_full = (
            sem("x1_full"), sem("gain_full"), sem("vec_full"), sem("tab_full"), sem("pool_w_full"))
        bias_stored, bias_full, out_stored = sem("bias_stored"), sem("bias_full"), sem("out_stored")
        hi_done, lo_done, unit_done = sem("hi_done"), sem("lo_done"), sem("unit_done")
        ident_done, prep_done, pads_done, pool_w_split = (
            sem("ident_done"), sem("prep_done"), sem("pads_done"), sem("pool_w_split"))
        vec_mm, vec_read = sem("vec_mm"), sem("vec_read")
        sq_done, pool_tick, rstd_done, xn_done, xt_done = (
            sem("sq_done"), sem("pool_tick"), sem("rstd_done"), sem("xn_done"), sem("xt_done"))
        h_hi_done, h_lo_done = sem("h_hi_done"), sem("h_lo_done")
        acc_act, acc_dve, qk_hi = sem("acc_act"), sem("acc_dve"), sem("qk_hi")
        s_full, s_read, exp_done, inv_done, p_ready = (
            sem("s_full"), sem("s_read"), sem("exp_done"), sem("inv_done"), sem("p_ready"))
        t_full, t_hi, t_read = sem("t_full"), sem("t_hi"), sem("t_read")
        vo_full, vo_hi, vo_read = sem("vo_full"), sem("vo_hi"), sem("vo_read")
        conv_step, ln_act, ln_dve, ln_mm, ln_rstd, d_done, br_split, br_mm, br_act, br_ready = (
            sem("conv_step"), sem("ln_act"), sem("ln_dve"), sem("ln_mm"), sem("ln_rstd"), sem("d_done"),
            sem("br_split"), sem("br_mm"), sem("br_act"), sem("br_ready"))
        mix_read, mix_sum, m_hi, m_lo = sem("mix_read"), sem("mix_sum"), sem("m_hi"), sem("m_lo")
        d0_full, d1_full, yg_done, x1_done, h2_hi, h2_lo, xt2_done = (
            sem("d0_full"), sem("d1_full"), sem("yg_done"), sem("x1_done"), sem("h2_hi"), sem("h2_lo"),
            sem("xt2_done"))
        tanh_done, g_read, u_read, f_hi_done, f_lo_done = (
            sem("tanh_done"), sem("g_read"), sem("u_read"), sem("f_hi_done"), sem("f_lo_done"))
        y1_full, y_gained, out_ready = sem("y1_full"), sem("y_gained"), sem("out_ready")

        block = ctx.enter_context(nc.Block())

        w_in_k = w_in[0].rearrange("(k p) n -> p k n", p=P)
        w_br_k = w_branch.rearrange("(k p) n -> p k n", p=P)
        w_out_k = w_out[0].rearrange("(k p) n -> p k n", p=P)
        w_up_k = w_ffn_in[0].rearrange("(k p) n -> p k n", p=P)
        w_dn_k = w_ffn_out[0].rearrange("(k p) n -> p k n", p=P)

        def k8(tile):
            return tile.rearrange("p (k c) -> p k c", k=8)

        def k2(tile):
            return tile.rearrange("p (k c) -> p k c", k=2)

        def pair_unit_freed(p, j):
            if j < 2:
                return acc_dve, 2 + 2 * p + j + 1
            return acc_act, 4 + 7 * p + (j - 2) + 1

        FIRST_FREED = [(acc_act, 1), (acc_dve, 1), (acc_act, 2), (acc_dve, 2), (acc_act, 3), (acc_act, 4)]

        @block.sync
        def _(sp):
            def load(u, slot, src, view):
                if not (isinstance(u, int) and u < RING):
                    sp.wait_ge(lo_done, u - RING + 1)
                sp.dma_start(view(raw[:, slot, :]), src).then_inc(raw_full[slot], 16)

            for t in range(TOK):
                sp.dma_start(x_tok[:, t, :], x[0, t * P:(t + 1) * P, :]).then_inc(x_full[t], 16)
            first = [COL_CONV + 256, COL_CONV, COL_CONV + 384, COL_CONV + 128, COL_POOL, COL_POOL + 128]
            for u, col in enumerate(first):
                load(u, u % RING, w_in_k[:, :, col:col + P], k8)

            def pair_loads(p):
                for j in range(PAIR_UNITS):
                    col = [COL_Q, COL_K, COL_V][j] + P * p if j < 3 else COL_GATE + 6 * P * p + P * (j - 3)
                    load(FIRST_UNITS + PAIR_UNITS * p + j, j % RING, w_in_k[:, :, bass.ds(col, P)], k8)
                    if j == 3:
                        src = bass.AP(bias_scratch.tensor, p * (2 * BIAS_LEN), [[1, P], [BIAS_LEN, 2], [1, SEQ]])
                        sp.dma_start(bias_h[:, :, :], src).then_inc(bias_full, 16)

            sp.wait_ge(bias_stored, 16)
            with sp.Fori(0, PAIRS) as p:
                pair_loads(p)
            for m in range(KT):
                u = U_MIX + m
                load(u, u % RING, w_br_k[:, :, m * P:(m + 1) * P], k8)
            for n in range(8):
                u = U_OUT + n
                half, kp = n // 4, n % 4
                load(u, u % RING, w_out_k[:, 2 * kp:2 * kp + 2, half * SEQ:(half + 1) * SEQ], k2)
                if n == 4:
                    sp.wait_ge(m_lo, KT)
                    sp.dma_start(x1[:, :, :], x[0].rearrange("(t p) d -> p t d", p=P)).then_inc(x1_full, 16)
                    sp.dma_start(gain[:, :], bass.AP(post_mix_g.tensor, 0, [[0, P], [1, D_MODEL]])).then_inc(gain_full, 16)
                    sp.dma_start(gain_ffn[:, :], bass.AP(pre_ffn_g.tensor, 0, [[0, P], [1, D_MODEL]])).then_inc(gain_full, 16)

            def ff_load(e, slot):
                j, odd = divmod(e, 2)
                load(U_FF + e, slot, w_up_k[:, :, odd * DFF + j * P:odd * DFF + (j + 1) * P], k8)

            for e in range(8):
                ff_load(e, (U_FF + e) % RING)
            sp.wait_ge(x1_done, TOK)
            sp.dma_start(gain[:, :], bass.AP(post_ffn_g.tensor, 0, [[0, P], [1, D_MODEL]])).then_inc(gain_full, 16)
            with sp.Fori(0, 3) as i:
                for jj in range(12):
                    col = i * (6 * P) + (jj % 2) * DFF + (4 + jj // 2) * P
                    load(U_FF + 8 + i * 12 + jj, (U_FF + 8 + jj) % RING, w_up_k[:, :, bass.ds(col, P)], k8)
            for n in range(FF_TILES):
                half, kp = divmod(n, FF_TILES // 2)
                u = U_DOWN + n
                load(u, u % RING, w_dn_k[:, 2 * kp:2 * kp + 2, half * SEQ:(half + 1) * SEQ], k2)
            for t in range(TOK):
                for half in range(2):
                    sp.wait_ge(out_ready, 2 * t + half + 1)
                    sp.dma_start(out[0, t * P:(t + 1) * P, half * SEQ:(half + 1) * SEQ],
                                 x1[:, t, half * SEQ:(half + 1) * SEQ]).then_inc(out_stored, 16)
            sp.wait_ge(out_stored, 16 * 2 * TOK)

        @block.gpsimd
        def _(pool):
            pool.memset(ident[:, :], 0.0).then_inc(pool_tick, 1)
            pool.wait_ge(pool_tick, 1)
            pool.affine_select(out=ident[:, :], in_=ident[:, :], compare_op=ALU.not_equal, fill=1.0, base=0,
                               pattern=[[-1, P]], channel_multiplier=1).then_inc(ident_done, 1)
            tick = 1

            def rsqrt(col_in, col_tmp, col_out, mult, eps):
                nonlocal tick
                pool.tensor_scalar(stat[:, col_tmp:col_tmp + 1], stat[:, col_in:col_in + 1], mult, eps,
                                   ALU.mult, ALU.add).then_inc(pool_tick, 1)
                tick += 1
                pool.wait_ge(pool_tick, tick)
                return pool.tensor_tensor(stat[:, col_out:col_out + 1], stat[:, col_tmp:col_tmp + 1],
                                          stat[:, 95:96], ALU.pow)

            pool.memset(stat[:, 88:96], -0.5).then_inc(pool_tick, 1)
            tick += 1
            pool.wait_ge(pool_tick, tick)
            for t in range(TOK):
                pool.wait_ge(sq_done, t + 1)
                rsqrt(t, 4 + t, 8 + t, 1.0 / D_MODEL, EPS).then_inc(rstd_done, 1)

            pool.memset(u_conv[:, :, 0:CONV_PAD], 0.0).then_inc(pads_done, 1)
            pool.memset(u_pool[:, :, 0:POOL_PAD], 0.0).then_inc(pads_done, 1)
            pool.wait_ge(pads_done, 2)
            pool.wait_ge(acc_act, 4)
            n = POOL_PAD + SEQ

            def link(ins):
                nonlocal tick
                ins.then_inc(pool_tick, 1)
                tick += 1
                pool.wait_ge(pool_tick, tick)

            link(pool.tensor_tensor(sum_a[:, :, 1:n], u_pool[:, :, 1:n], u_pool[:, :, 0:n - 1], ALU.add))
            link(pool.tensor_tensor(sum_b[:, :, 3:n], sum_a[:, :, 3:n], sum_a[:, :, 1:n - 2], ALU.add))
            link(pool.tensor_tensor(sum_a[:, 1, 7:n], sum_b[:, 1, 7:n], sum_b[:, 1, 3:n - 4], ALU.add))
            link(pool.tensor_tensor(sum_b[64:P, 1, 15:n], sum_a[64:P, 1, 15:n], sum_a[64:P, 1, 7:n - 8], ALU.add))
            ratio = const[:, C_RATIO:C_RATIO + 32].rearrange("p (c t) -> p c t", c=2)
            for lo, s in ((0, sum_a), (64, sum_b)):
                rows = slice(lo, lo + 64)
                link(pool.tensor_tensor(s[rows, :, POOL_PAD:POOL_PAD + 16], s[rows, :, POOL_PAD:POOL_PAD + 16],
                                        ratio[rows, :, :], ALU.mult))
                for c in range(2):
                    link(pool.tensor_scalar(s[rows, c, POOL_PAD:n], s[rows, c, POOL_PAD:n],
                                            const[rows, C_INV + c:C_INV + c + 1], None, ALU.mult))
                pool.tensor_tensor(d_pool[rows, :, :], s[rows, :, POOL_PAD:n], u_pool[rows, :, POOL_PAD:n],
                                   ALU.subtract).then_inc(d_done, 1)
            pool.wait_ge(ln_dve, 5)
            pool.tensor_tensor(stat[:, 68:72], stat[:, 64:68], stat[:, 88:92], ALU.pow).then_inc(ln_rstd, 1)
            for m in range(KT):
                b = m % 2
                pool.wait_ge(mix_read, m + 1)
                link(pool.tensor_tensor(mix[:, b, 0, :], mix[:, b, 0, :], mix[:, b, 1, :], ALU.add))
                pool.tensor_tensor(mix[:, b, 0, :], mix[:, b, 0, :], mix[:, b, 2, :], ALU.add).then_inc(mix_sum, 1)
            for t in range(TOK):
                pool.wait_ge(sq_done, 4 + 4 + 2 * t + 1)
                link(pool.tensor_tensor(stat[:, 24 + t:25 + t], stat[:, 12 + t:13 + t], stat[:, 16 + t:17 + t], ALU.add))
                rsqrt(24 + t, 28 + t, 32 + t, 1.0 / D_MODEL, 4 * EPS).then_inc(rstd_done, 1)
                pool.wait_ge(sq_done, 4 + 4 + 2 * t + 2)
                rsqrt(20 + t, 36 + t, 40 + t, 1.0 / D_MODEL, EPS).then_inc(rstd_done, 1)
            for t in range(TOK):
                pool.wait_ge(sq_done, 16 + 4 + t + 1)
                link(pool.tensor_tensor(stat[:, 52 + t:53 + t], stat[:, 44 + t:45 + t], stat[:, 48 + t:49 + t], ALU.add))
                rsqrt(52 + t, 56 + t, 60 + t, 1.0 / D_MODEL, EPS).then_inc(rstd_done, 1)

        @block.scalar
        def _(act):
            def hi(u, slot):
                act.wait_ge(raw_full[slot], _raw_count(u, slot))
                if not (isinstance(u, int) and u < RING):
                    act.wait_ge(unit_done, in_ring(u) - RING + 1 if isinstance(u, int) else u)
                act.activation(w_hi[:, ring_slot(u, slot), :], raw[:, slot, :], ACT.Copy).then_inc(hi_done, 1)

            def ring_slot(u, slot):
                return in_ring(u) % RING

            def hi_at(u, slot, hslot, loads, done):
                act.wait_ge(raw_full[slot], loads)
                act.wait_ge(unit_done, done)
                act.activation(w_hi[:, hslot, :], raw[:, slot, :], ACT.Copy).then_inc(hi_done, 1)

            act.dma_start(onehot_sb[0:33, :], onehot).then_inc(tab_full, 16)
            act.dma_start(table[0:32, :], rel_bias).then_inc(tab_full, 16)
            act.dma_start(vec[:, :], vecs).then_inc(vec_full, 16)
            act.dma_start(const[:, :], pool_const).then_inc(vec_full, 16)
            act.wait_ge(prep_done, 1)
            for g in range(4):
                r0, c = (g % 2) * 64, g // 2
                act.dma_start(pool_w[r0:r0 + 64, c, r0:r0 + 64], w_pool_g[0, g]).then_inc(pool_w_full, 16)
            act.wait_ge(vec_mm, 1)
            act.activation(bias_vec[0:8, 0:SEQ], bank[0][0:8, :], ACT.Copy).then_inc(vec_read, 1)
            act.activation(bias_vec[0:8, SEQ:BIAS_LEN], bank[1][0:8, 0:P], ACT.Copy).then_inc(vec_read, 1)
            act.wait_ge(vec_read, 2)
            act.dma_start(bias_scratch, bias_vec[0:8, :]).then_inc(bias_stored, 16)

            nsq = 0

            def square_sum(in_, col, scrap):
                nonlocal nsq
                if nsq:
                    act.wait_ge(sq_done, nsq)
                nsq += 1
                act.activation(scrap, in_, ACT.Square, accum_out=stat[:, col:col + 1]).then_inc(sq_done, 1)

            for t in range(TOK):
                act.wait_ge(x_full[t], 16)
                square_sum(x_tok[:, t, :], t, junk_x[:, :])
            hi(0, 0)
            act.wait_ge(vec_full, 32)
            act.wait_ge(xt_done, TOK)
            for k in range(KT):
                act.activation(h_hi[:, k, :], bank[k][:, :], ACT.Copy, scale=vec[:, V_PRE + k:V_PRE + k + 1])\
                   .then_inc(h_hi_done, 1)
            hi(1, 1)
            act.wait_ge(pool_w_full, 64)
            act.activation(pool_w_hi[:, :, :], pool_w[:, :, :], ACT.Copy).then_inc(pool_w_split, 1)

            for u in range(FIRST_UNITS):
                hi(u + 2, (u + 2) % RING)
                if u in (0, 2):
                    act.wait_ge(unit_done, u + 1)
                    act.activation(conv_gate[:, u // 2, :], bank[u % RING][:, :], ACT.Tanh, scale=0.5).then_inc(acc_act, 1)
                if u >= 4:
                    act.wait_ge(unit_done, u + 1)
                    act.activation(u_pool[:, u - 4, POOL_PAD:], bank[u % RING][:, :], ACT.Copy).then_inc(acc_act, 1)

            def exp(p, i):
                w = (i % 4 + 1) * P
                act.wait_ge(s_read, 8 * p + i + 1)
                if i >= 2:
                    act.wait_ge(t_full, 8 * p + i - 1)
                act.activation(prob[:, i % 2, 0:w], neg_logit[:, i % 2, 0:w], ACT.Exp, bias=neg_max[:, i:i + 1],
                               scale=-1.0, accum_out=row_sum[:, i:i + 1]).then_inc(exp_done, 1)

            def pT_hi_part(p, i):
                qt = i % 4
                act.wait_ge(t_full, 8 * p + i + 1)
                if i >= 4:
                    act.wait_ge(vo_full, 3 * p + 2)
                act.activation(pT_hi[:, 0:qt + 1, qt * P:(qt + 1) * P],
                               bank[5 + i % 2][:, 0:(qt + 1) * P].rearrange("p (k c) -> p k c", c=P),
                               ACT.Copy).then_inc(t_hi, 1)

            def v_hi_part(p):
                act.wait_ge(vo_full, 3 * p + 1)
                act.activation(v_hi[:, :], bank[7][:, :], ACT.Copy).then_inc(vo_hi, 1)

            def o_hi_part(p, head):
                act.wait_ge(vo_full, 3 * p + 2 + head)
                rows = slice(HEAD * head, HEAD * head + HEAD)
                act.activation(br_hi[rows, p, :], bank[7][rows, :], ACT.Copy).then_inc(vo_hi, 1)

            def pair_steps(p, last):
                for j in range(PAIR_UNITS):
                    u = FIRST_UNITS + PAIR_UNITS * p + j
                    hi_at(u + 2, (j + 2) % RING, (j + 2) % RING, 16 * (3 * p + 3 + (j + 2) // 3), u)
                    if j == 3:
                        exp(p, 0)
                        exp(p, 1)
                    if j == 4:
                        v_hi_part(p)
                        pT_hi_part(p, 0)
                        pT_hi_part(p, 1)
                        exp(p, 2)
                        exp(p, 3)
                    if j == 5:
                        pT_hi_part(p, 2)
                        pT_hi_part(p, 3)
                        exp(p, 4)
                        exp(p, 5)
                    if j == 6:
                        o_hi_part(p, 0)
                        pT_hi_part(p, 4)
                        pT_hi_part(p, 5)
                        exp(p, 6)
                        exp(p, 7)
                    if j == 7:
                        pT_hi_part(p, 6)
                        pT_hi_part(p, 7)
                    if j == 8:
                        o_hi_part(p, 1)
                    if last:
                        branch_steps(j)
                    act.wait_ge(unit_done, u + 1)
                    if j == 0:
                        act.activation(qT_hi[:, :], bank[j % RING][:, :], ACT.Copy).then_inc(qk_hi, 1)
                    elif j == 1:
                        act.activation(kT_hi[:, :], bank[j % RING][:, :], ACT.Copy).then_inc(qk_hi, 1)
                    elif j == 2:
                        act.activation(vT[:, :], bank[j % RING][:, :], ACT.Copy).then_inc(acc_act, 1)
                    else:
                        g = 6 * p + (j - 3)
                        act.activation(gate[:, g, :], bank[j % RING][:, :], ACT.Tanh, scale=0.5,
                                       bias=half_bias[:, bass.ds(g, 1)]).then_inc(acc_act, 1)

            def branch_steps(j):
                if j == 0:
                    act.wait_ge(conv_step, 2 * CONV_K)
                    act.wait_ge(d_done, 2)
                    act.activation(t1[:, :, :], conv_acc[:, :, :], ACT.Copy).then_inc(ln_act, 1)
                if j == 1:
                    act.wait_ge(ln_dve, 2)
                    act.activation(t3[:, :, :], conv_acc[:, :, :], ACT.Square).then_inc(ln_act, 1)
                    act.wait_ge(ln_act, 2)
                    act.activation(t1[:, :, :], t3[:, :, :], ACT.Copy).then_inc(ln_act, 1)
                if j == 7:
                    act.wait_ge(ln_dve, 7)
                    for c in range(2):
                        act.activation(conv_acc[:, c, :], conv_acc[:, c, :], ACT.Identity,
                                       scale=vec[:, V_LNG + c:V_LNG + c + 1],
                                       bias=vec[:, V_LNB + c:V_LNB + c + 1]).then_inc(ln_act, 1)
                    act.wait_ge(ln_act, 6)
                    act.activation(t3[:, :, :], conv_acc[:, :, :], ACT.Tanh, scale=0.5).then_inc(ln_act, 1)
                if j == 6:
                    act.activation(t1[:, :, :], d_pool[:, :, :], ACT.Copy).then_inc(ln_act, 1)
                if j == 8:
                    act.wait_ge(ln_dve, 9)
                    act.activation(br_hi[:, 6:8, :], t3[:, :, :], ACT.Copy, scale=0.5).then_inc(br_act, 1)
                if j == 8:
                    for c in range(2):
                        act.wait_ge(br_mm, c + 1)
                        act.activation(br_hi[:, 4 + c, :], bank[5 + c][:, :], ACT.Copy,
                                       scale=vec[:, V_PSCALE + c:V_PSCALE + c + 1]).then_inc(br_act, 1)

            with act.Fori(0, PAIRS - 1) as p:
                pair_steps(p, False)
            pair_steps(PAIRS - 1, True)

            def merged_hi(m):
                act.wait_ge(mix_sum, m + 1)
                act.activation(h_hi[:, m, :], mix[:, m % 2, 0, :], ACT.Copy).then_inc(m_hi, 1)

            def wo_hi_part(n):
                u = U_OUT + n
                half, kp = divmod(n, 4)
                act.wait_ge(raw_full[u % RING], 16 * (u // RING + 1))
                act.activation(wo_hi[half][:, 2 * kp:2 * kp + 2, :], k2(raw[:, u % RING, :]), ACT.Copy).then_inc(hi_done, 1)

            def hi_int(u):
                hi_at(u, u % RING, in_ring(u) % RING, 16 * (u // RING + 1), in_ring(u) - RING + 1)

            for m in range(KT):
                u = U_MIX + m
                if u + 2 < U_OUT:
                    hi_int(u + 2)
                else:
                    act.wait_ge(vo_full, 12)
                    wo_hi_part(u + 2 - U_OUT)
                if m:
                    merged_hi(m - 1)
            wo_hi_part(2)
            merged_hi(7)
            wo_hi_part(3)
            act.wait_ge(mix_read, KT)
            for n in range(4, 8):
                wo_hi_part(n)
            for e in range(3):
                hi_int(U_FF + e)
            act.wait_ge(m_lo, KT)
            for t in range(TOK):
                act.wait_ge(d0_full, t + 1)
                square_sum(bank[D0[t]][:, :], 12 + t, junk[:, 0:SEQ])

            def sq_y(t):
                act.wait_ge(d1_full, t + 1)
                square_sum(bank[D1[t]][:, :], 16 + t, junk[:, 0:SEQ])

            def sq_x(t):
                act.wait_ge(x1_done, t + 1)
                square_sum(x1[:, t, :], 20 + t, junk[:, :])

            def h2_hi_part(t):
                act.wait_ge(xt2_done, t + 1)
                for q, b in enumerate((D0[t], D1[t])):
                    act.activation(h_hi[:, 4 * q:4 * q + 4, t * P:(t + 1) * P],
                                   bank[b][:, :].rearrange("p (k c) -> p k c", c=P), ACT.Copy).then_inc(h2_hi, 1)

            sq_y(0)
            sq_x(0)
            sq_y(1)
            sq_x(1)
            sq_y(2)
            h2_hi_part(0)
            sq_x(2)
            sq_y(3)
            h2_hi_part(1)
            sq_x(3)
            h2_hi_part(2)
            h2_hi_part(3)

            def f_hi_part(j, b):
                act.wait_ge(u_read, j + 1)
                act.activation(f_hi[:, j, :], ff_prod[:, b, :], ACT.Copy).then_inc(f_hi_done, 1)

            def ff_tanh_part(j, b, g_bank):
                act.wait_ge(unit_done, 2 * j + (in_ring(U_FF) + 1))
                if not isinstance(j, int) or j >= 2:
                    act.wait_ge(g_read, j - 1)
                act.activation(ff_tanh[:, b, :], bank[g_bank][:, :], ACT.Tanh, scale=0.5).then_inc(tanh_done, 1)

            for e in range(8):
                if e >= 1:
                    hi_int(U_FF + 2 + e)
                if e % 2 == 0:
                    j = e // 2
                    if j:
                        f_hi_part(j - 1, (j - 1) % 2)
                    ff_tanh_part(j, j % 2, FFB[e % 4])
            with act.Fori(0, 3) as i:
                for jj in range(12):
                    u0 = U_FF + 10 + jj
                    hi_at(None, u0 % RING, in_ring(u0) % RING, i * 64 + 16 * (u0 // RING + 1),
                          i * 12 + (in_ring(u0) - RING + 1))
                    if jj % 2 == 0:
                        j = i * 6 + (4 + jj // 2)
                        f_hi_part(j - 1, (3 + jj // 2) % 2)
                        ff_tanh_part(j, (jj // 2) % 2, FFB[jj % 4])
            f_hi_part(FF_TILES - 1, 1)
            for n in range(2, FF_TILES):
                hi_int(U_DOWN + n)
                if n == 13:
                    act.wait_ge(unit_done, in_ring(U_DOWN) + 11)
                    for t in range(TOK):
                        square_sum(bank[Y0[t]][:, :], 44 + t, junk[:, 0:SEQ])
            for t in range(TOK):
                act.wait_ge(y1_full, t + 1)
                square_sum(bank[Y1[t]][:, :], 48 + t, junk[:, 0:SEQ])

        @block.vector
        def _(dve):
            def lo(dst, slot, src_hi, count):
                dve.wait_ge(hi_done, count)
                dve.tensor_tensor(dst, src_hi[0], src_hi[1], ALU.subtract).then_inc(lo_done, 1)

            def lo_at(slot, hslot, count):
                lo(w_lo[:, hslot, :], slot, (raw[:, slot, :], w_hi[:, hslot, :].bitcast(F32)), count)

            def lo_int(u):
                lo_at(u % RING, in_ring(u) % RING, u + 1)

            def wo_lo_part(n):
                u = U_OUT + n
                half, kp = divmod(n, 4)
                ks = slice(2 * kp, 2 * kp + 2)
                lo(wo_lo[half][:, ks, :], u % RING, (k2(raw[:, u % RING, :]), wo_hi[half][:, ks, :].bitcast(F32)), u + 1)

            dve.memset(pool_w[:, :, :], 0.0).then_inc(prep_done, 1)
            dve.memset(mean_w[:, :].bitcast(F32), 1.0 / 256).then_inc(prep_done, 1)
            dve.memset(table[32:33, :], 8 * MASKED).then_inc(prep_done, 1)
            dve.wait_ge(tab_full, 32)
            dve.tensor_scalar(table[0:32, :], table[0:32, :], 8.0, None, ALU.mult).then_inc(prep_done, 1)
            dve.wait_ge(vec_full, 32)
            dve.tensor_scalar(half_bias[:, :], vec[:, V_GATE:V_GATE + GATES], 0.5, None, ALU.mult).then_inc(prep_done, 1)
            dve.tensor_scalar(half_dw[:, :], vec[:, V_DW:V_DW + 2 * CONV_K], 0.5, None, ALU.mult).then_inc(prep_done, 1)
            for t in range(TOK):
                dve.wait_ge(rstd_done, t + 1)
                dve.tensor_scalar(x_tok[:, t, :], x_tok[:, t, :], stat[:, 8 + t:9 + t], None, ALU.mult).then_inc(xn_done, 1)
            lo_int(0)
            for k in range(KT):
                dve.wait_ge(h_hi_done, k + 1)
                dve.scalar_tensor_tensor(out=h_lo[:, k, :], in0=bank[k][:, :], scalar=vec[:, V_PRE + k:V_PRE + k + 1],
                                         in1=h_hi[:, k, :].bitcast(F32), op0=ALU.mult, op1=ALU.subtract)\
                   .then_inc(h_lo_done, 1)
            lo_int(1)
            dve.wait_ge(pool_w_split, 1)
            dve.tensor_tensor(pool_w_lo[:, :, :], pool_w[:, :, :], pool_w_hi[:, :, :].bitcast(F32), ALU.subtract)\
               .then_inc(pool_w_split, 1)
            for u in range(FIRST_UNITS):
                lo_int(u + 2)
                if u in (1, 3):
                    c = u // 2
                    dve.wait_ge(unit_done, u + 1)
                    dve.wait_ge(acc_act, c + 1)
                    dve.scalar_tensor_tensor(out=u_conv[:, c, CONV_PAD:], in0=conv_gate[:, c, :], scalar=1.0,
                                             in1=bank[u % RING][:, :], op0=ALU.add, op1=ALU.mult).then_inc(acc_dve, 1)
                if u == 4:
                    dve.wait_ge(acc_dve, 2)
                    dve.wait_ge(prep_done, 6)
                    for c in range(2):
                        w = c * CONV_K + CONV_K - 1
                        dve.tensor_scalar(conv_acc[:, c, :], u_conv[:, c, CONV_PAD:], half_dw[:, w:w + 1],
                                          vec[:, V_BDW + c:V_BDW + c + 1], ALU.mult, ALU.add).then_inc(conv_step, 1)
            dve.wait_ge(pads_done, 2)

            def taps(p, s0):
                for s in (s0, s0 + 1):
                    tap = 10 * p + s
                    for c in range(2):
                        dve.wait_ge(conv_step, 2 * tap + (2 + c - 1))
                        dve.scalar_tensor_tensor(out=conv_acc[:, c, :], in0=u_conv[:, c, bass.ds(tap + 2, SEQ)],
                                                 scalar=half_dw[:, bass.ds(tap + c * CONV_K, 1)],
                                                 in1=conv_acc[:, c, :], op0=ALU.mult, op1=ALU.add).then_inc(conv_step, 1)

            def logits(p, i):
                head, w = i // 4, (i % 4 + 1) * P
                if i == 0:
                    dve.wait_ge(bias_full, 16 * p + 16)
                if i >= 2:
                    dve.wait_ge(exp_done, 8 * p + i - 1)
                dve.wait_ge(s_full, 8 * p + i + 1)
                dve.memset(spare[:, i:i + 1], 0.0)
                dve.tensor_tensor_reduce(neg_logit[:, i % 2, 0:w], bank[3 + i % 2][:, 0:w],
                                         bias_h[:, head, w - 1::-1], -0.125, 3e38, ALU.add, ALU.min,
                                         neg_max[:, i:i + 1]).then_inc(s_read, 1)

            def normalise(p, g):
                dve.wait_ge(exp_done, 8 * p + 2 * g + 2)
                dve.reciprocal(row_inv[:, 2 * g:2 * g + 2], row_sum[:, 2 * g:2 * g + 2]).then_inc(inv_done, 1)
                dve.wait_ge(inv_done, 4 * p + g + 1)
                for i in (2 * g, 2 * g + 1):
                    w = (i % 4 + 1) * P
                    dve.tensor_scalar(prob[:, i % 2, 0:w], prob[:, i % 2, 0:w], row_inv[:, i:i + 1], None, ALU.mult)\
                       .then_inc(p_ready, 1)

            def pT_lo_part(p, i):
                qt = i % 4
                dve.wait_ge(t_hi, 8 * p + i + 1)
                dve.tensor_tensor(pT_lo[:, 0:qt + 1, qt * P:(qt + 1) * P],
                                  bank[5 + i % 2][:, 0:(qt + 1) * P].rearrange("p (k c) -> p k c", c=P),
                                  pT_hi[:, 0:qt + 1, qt * P:(qt + 1) * P].bitcast(F32), ALU.subtract).then_inc(t_read, 1)

            def v_lo_part(p):
                dve.wait_ge(vo_hi, 3 * p + 1)
                dve.tensor_tensor(v_lo[:, :], bank[7][:, :], v_hi[:, :].bitcast(F32), ALU.subtract).then_inc(vo_read, 1)

            def o_lo_part(p, head):
                dve.wait_ge(vo_hi, 3 * p + 2 + head)
                rows = slice(HEAD * head, HEAD * head + HEAD)
                dve.tensor_tensor(br_lo[rows, p, :], bank[7][rows, :], br_hi[rows, p, :].bitcast(F32), ALU.subtract)\
                   .then_inc(vo_read, 1)

            def pair_steps(p, last):
                for j in range(PAIR_UNITS):
                    lo_at((j + 2) % RING, (j + 2) % RING, PAIR_UNITS * p + (FIRST_UNITS + j + 3))
                    if j == 3:
                        logits(p, 0)
                        logits(p, 1)
                        normalise(p, 0)
                    if j == 4:
                        logits(p, 2)
                        logits(p, 3)
                        v_lo_part(p)
                        pT_lo_part(p, 0)
                        pT_lo_part(p, 1)
                        normalise(p, 1)
                    if j == 5:
                        logits(p, 4)
                        logits(p, 5)
                        pT_lo_part(p, 2)
                        pT_lo_part(p, 3)
                        normalise(p, 2)
                    if j == 6:
                        logits(p, 6)
                        logits(p, 7)
                        o_lo_part(p, 0)
                        pT_lo_part(p, 4)
                        pT_lo_part(p, 5)
                        normalise(p, 3)
                    if j == 7:
                        pT_lo_part(p, 6)
                        pT_lo_part(p, 7)
                    if j == 8:
                        o_lo_part(p, 1)
                    if last:
                        branch_steps(j)
                    elif j in (0, 1, 2, 7, 8):
                        taps(p, {0: 0, 1: 2, 2: 4, 7: 6, 8: 8}[j])
                    if j < 2:
                        dst, part = ((qT_lo, qT_hi), (kT_lo, kT_hi))[j]
                        dve.wait_ge(qk_hi, 2 * p + j + 1)
                        dve.tensor_tensor(dst[:, :], bank[j % RING][:, :], part[:, :].bitcast(F32), ALU.subtract)\
                           .then_inc(acc_dve, 1)

            def over_tiles(ap):
                return ap.rearrange("p (a t) -> p a t", a=1).to_broadcast([P, 2, SEQ])

            def branch_steps(j):
                if j == 0:
                    dve.wait_ge(ln_act, 1)
                    dve.tensor_tensor(t2[:, :, :], conv_acc[:, :, :], t1[:, :, :].bitcast(F32), ALU.subtract)\
                       .then_inc(ln_dve, 1)
                if j == 1:
                    dve.wait_ge(ln_mm, 1)
                    for c in range(2):
                        ins = dve.tensor_tensor(conv_acc[:, c, :], conv_acc[:, c, :], bank[5][:, :], ALU.subtract)
                    ins.then_inc(ln_dve, 1)
                    dve.wait_ge(ln_act, 3)
                    dve.tensor_tensor(t2[:, :, :], t3[:, :, :], t1[:, :, :].bitcast(F32), ALU.subtract)\
                       .then_inc(ln_dve, 1)
                if j == 3:
                    dve.wait_ge(ln_mm, 2)
                    dve.tensor_scalar(t3[:, 0, :], bank[6][:, :], EPS, None, ALU.add).then_inc(ln_dve, 1)
                if j == 5:
                    dve.wait_ge(ln_mm, 3)
                    dve.tensor_copy(stat[:, 64:68], bank[7][:, 0:SEQ:P]).then_inc(ln_dve, 1)
                    dve.wait_ge(ln_rstd, 1)
                    dve.tensor_copy(t3[:, 1, :].rearrange("p (t c) -> p t c", c=P),
                                    stat[:, 68:72].rearrange("p (t c) -> p t c", c=1).to_broadcast([P, TOK, P]))\
                       .then_inc(ln_dve, 1)
                if j == 6:
                    dve.wait_ge(ln_act, 4)
                    dve.tensor_tensor(t2[:, :, :], d_pool[:, :, :], t1[:, :, :].bitcast(F32), ALU.subtract)\
                       .then_inc(br_split, 1)
                if j == 7:
                    dve.wait_ge(ln_mm, 4)
                    for c in range(2):
                        ins = dve.tensor_tensor(conv_acc[:, c, :], conv_acc[:, c, :], bank[7][:, :], ALU.mult)
                    ins.then_inc(ln_dve, 1)
                if j == 8:
                    dve.wait_ge(ln_act, 7)
                    dve.scalar_tensor_tensor(out=t3[:, :, :], in0=t3[:, :, :], scalar=1.0, in1=conv_acc[:, :, :],
                                             op0=ALU.add, op1=ALU.mult).then_inc(ln_dve, 2)
                if j == 8:
                    dve.wait_ge(br_act, 1)
                    dve.wait_ge(ln_dve, 9)
                    dve.scalar_tensor_tensor(out=br_lo[:, 6:8, :], in0=t3[:, :, :], scalar=0.5,
                                             in1=br_hi[:, 6:8, :].bitcast(F32), op0=ALU.mult, op1=ALU.subtract)\
                       .then_inc(br_ready, 1)
                    for c in range(2):
                        dve.wait_ge(br_act, 2 + c)
                        dve.scalar_tensor_tensor(out=br_lo[:, 4 + c, :], in0=bank[5 + c][:, :],
                                                 scalar=vec[:, V_PSCALE + c:V_PSCALE + c + 1],
                                                 in1=br_hi[:, 4 + c, :].bitcast(F32), op0=ALU.mult,
                                                 op1=ALU.subtract).then_inc(br_ready, 1)

            with dve.Fori(0, PAIRS - 1) as p:
                pair_steps(p, False)
            pair_steps(PAIRS - 1, True)

            def merged_lo(m):
                dve.wait_ge(m_hi, m + 1)
                dve.tensor_tensor(h_lo[:, m, :], mix[:, m % 2, 0, :], h_hi[:, m, :].bitcast(F32), ALU.subtract)\
                   .then_inc(m_lo, 1)

            for m in range(KT):
                u = U_MIX + m
                if u + 2 < U_OUT:
                    lo_int(u + 2)
                else:
                    wo_lo_part(u + 2 - U_OUT)
                if m:
                    merged_lo(m - 1)
                dve.wait_ge(unit_done, u + 1)
                for i in range(3):
                    ins = dve.scalar_tensor_tensor(out=mix[:, m % 2, i, :], in0=gate[:, KT * i + m, :], scalar=1.0,
                                                   in1=bank[3 * (m % 2) + i][:, :], op0=ALU.add, op1=ALU.mult)
                ins.then_inc(mix_read, 1)
            wo_lo_part(2)
            merged_lo(7)
            wo_lo_part(3)
            for n in range(4, 8):
                wo_lo_part(n)
            for e in range(3):
                lo_int(U_FF + e)

            def residual(t):
                if t == 0:
                    dve.wait_ge(gain_full, 32)
                    dve.wait_ge(x1_full, 16)
                else:
                    dve.wait_ge(x1_done, t)
                dve.wait_ge(sq_done, 4 + 4 + 2 * t + 1)
                dve.tensor_tensor(y_gain[:, 0:SEQ], bank[D0[t]][:, :], gain[:, 0:SEQ], ALU.mult).then_inc(yg_done, 1)
                dve.tensor_tensor(y_gain[:, SEQ:], bank[D1[t]][:, :], gain[:, SEQ:], ALU.mult).then_inc(yg_done, 1)
                dve.wait_ge(yg_done, 2 * t + 2)
                dve.wait_ge(rstd_done, TOK + 2 * t + 1)
                dve.scalar_tensor_tensor(out=x1[:, t, :], in0=y_gain[:, :], scalar=stat[:, 32 + t:33 + t],
                                         in1=x1[:, t, :], op0=ALU.mult, op1=ALU.add).then_inc(x1_done, 1)

            def norm_x1(t):
                dve.wait_ge(rstd_done, TOK + 2 * t + 2)
                if t >= 2:
                    dve.wait_ge(xt2_done, t - 1)
                dve.scalar_tensor_tensor(out=xn[:, t % 2, :], in0=x1[:, t, :], scalar=stat[:, 40 + t:41 + t],
                                         in1=gain_ffn[:, :], op0=ALU.mult, op1=ALU.mult).then_inc(xn_done, 1)

            def h2_lo_part(t):
                for q, b in enumerate((D0[t], D1[t])):
                    dve.wait_ge(h2_hi, 2 * t + q + 1)
                    dve.tensor_tensor(h_lo[:, 4 * q:4 * q + 4, t * P:(t + 1) * P],
                                      bank[b][:, :].rearrange("p (k c) -> p k c", c=P),
                                      h_hi[:, 4 * q:4 * q + 4, t * P:(t + 1) * P].bitcast(F32), ALU.subtract)\
                       .then_inc(h2_lo, 1)

            residual(0)
            norm_x1(0)
            residual(1)
            norm_x1(1)
            residual(2)
            h2_lo_part(0)
            norm_x1(2)
            residual(3)
            h2_lo_part(1)
            norm_x1(3)
            h2_lo_part(2)
            h2_lo_part(3)

            def f_lo_part(j, b):
                dve.wait_ge(f_hi_done, j + 1)
                dve.tensor_tensor(f_lo[:, j, :], ff_prod[:, b, :], f_hi[:, j, :].bitcast(F32), ALU.subtract)\
                   .then_inc(f_lo_done, 1)

            def silu_part(j, b, g_bank):
                dve.wait_ge(tanh_done, j + 1)
                if not isinstance(j, int) or j >= 2:
                    dve.wait_ge(u_read, j - 1)
                dve.scalar_tensor_tensor(out=ff_silu[:, b, :], in0=ff_tanh[:, b, :], scalar=1.0,
                                         in1=bank[g_bank][:, :], op0=ALU.add, op1=ALU.mult).then_inc(g_read, 1)

            def prod_part(j, b, u_bank):
                dve.wait_ge(unit_done, 2 * j + (in_ring(U_FF) + 2))
                dve.wait_ge(g_read, j + 1)
                if not isinstance(j, int) or j >= 2:
                    dve.wait_ge(f_lo_done, j - 1)
                dve.scalar_tensor_tensor(out=ff_prod[:, b, :], in0=ff_silu[:, b, :], scalar=0.5,
                                         in1=bank[u_bank][:, :], op0=ALU.mult, op1=ALU.mult).then_inc(u_read, 1)

            for e in range(8):
                j = e // 2
                if e >= 1:
                    lo_int(U_FF + 2 + e)
                if e % 2 == 0:
                    if j:
                        f_lo_part(j - 1, (j - 1) % 2)
                    silu_part(j, j % 2, FFB[e % 4])
                else:
                    prod_part(j, j % 2, FFB[e % 4])
            with dve.Fori(0, 3) as i:
                for jj in range(12):
                    u0 = U_FF + 10 + jj
                    lo_at(u0 % RING, in_ring(u0) % RING, i * 12 + (u0 + 1))
                    j = i * 6 + (4 + jj // 2)
                    if jj % 2 == 0:
                        f_lo_part(j - 1, (3 + jj // 2) % 2)
                        silu_part(j, (jj // 2) % 2, FFB[jj % 4])
                    else:
                        prod_part(j, (jj // 2) % 2, FFB[jj % 4])
            f_lo_part(FF_TILES - 1, 1)
            for n in range(2, FF_TILES):
                lo_int(U_DOWN + n)
                if n == 13:
                    dve.wait_ge(gain_full, 48)
                    for t in range(TOK):
                        dve.wait_ge(sq_done, 16 + t + 1)
                        dve.tensor_tensor(yg0[:, t, :], bank[Y0[t]][:, :], gain[:, 0:SEQ], ALU.mult).then_inc(y_gained, 1)
            for t in range(TOK):
                dve.wait_ge(sq_done, 20 + t + 1)
                if t >= 2:
                    dve.wait_ge(out_ready, 2 * t - 2)
                dve.tensor_tensor(yg1[:, t % 2, :], bank[Y1[t]][:, :], gain[:, SEQ:], ALU.mult).then_inc(y_gained, 1)
                dve.wait_ge(rstd_done, 12 + t + 1)
                r = stat[:, 60 + t:61 + t]
                dve.wait_ge(y_gained, 4 + t + 1)
                dve.scalar_tensor_tensor(out=x1[:, t, 0:SEQ], in0=yg0[:, t, :], scalar=r, in1=x1[:, t, 0:SEQ],
                                         op0=ALU.mult, op1=ALU.add).then_inc(out_ready, 1)
                dve.scalar_tensor_tensor(out=x1[:, t, SEQ:], in0=yg1[:, t % 2, :], scalar=r, in1=x1[:, t, SEQ:],
                                         op0=ALU.mult, op1=ALU.add).then_inc(out_ready, 1)

        @block.tensor
        def _(pe):
            def mm3(dst, a_hi, a_lo, b_hi, b_lo, start, stop):
                pe.matmul(dst, a_hi, b_hi, start=start, stop=False)
                pe.matmul(dst, a_hi, b_lo, start=False, stop=False)
                return pe.matmul(dst, a_lo, b_hi, start=False, stop=stop)

            def unit(slot, dst, m_hi_, m_lo_, before_k=None, cols=slice(0, SEQ)):
                for k in range(KT):
                    if before_k:
                        before_k(k)
                    ins = mm3(dst[:, cols], w_hi[:, slot, k * P:(k + 1) * P], w_lo[:, slot, k * P:(k + 1) * P],
                              m_hi_[:, k, cols], m_lo_[:, k, cols], k == 0, k == KT - 1)
                return ins

            pe.wait_ge(prep_done, 4)
            pe.matmul(bank[0][0:8, :], table[0:33, :], onehot_sb[0:33, 0:SEQ], start=True, stop=True)
            pe.matmul(bank[1][0:8, 0:P], table[0:33, :], onehot_sb[0:33, SEQ:BIAS_LEN], start=True, stop=True)\
              .then_inc(vec_mm, 1)
            pe.wait_ge(ident_done, 1)
            pe.wait_ge(vec_read, 2)
            for t in range(TOK):
                pe.wait_ge(xn_done, t + 1)
                for k in range(KT):
                    ins = pe.transpose(bank[k][:, t * P:(t + 1) * P], x_tok[:, t, k * P:(k + 1) * P], ident[:, :])
                ins.then_inc(xt_done, 1)
            for u in range(FIRST_UNITS):
                pe.wait_ge(lo_done, u + 1)
                if u >= RING:
                    pe.wait_ge(*FIRST_FREED[u - RING])
                unit(u % RING, bank[u % RING], h_hi, h_lo,
                     before_k=(lambda k: pe.wait_ge(h_lo_done, k + 1)) if u == 0 else None).then_inc(unit_done, 1)

            def scores(p, i):
                head, qt = divmod(i, 4)
                w = (qt + 1) * P
                rows, q = slice(HEAD * head, HEAD * head + HEAD), slice(qt * P, qt * P + P)
                if i >= 2:
                    pe.wait_ge(s_read, 8 * p + i - 1)
                mm3(bank[3 + i % 2][:, 0:w], qT_hi[rows, q], qT_lo[rows, q], kT_hi[rows, 0:w], kT_lo[rows, 0:w],
                    True, True).then_inc(s_full, 1)

            def turn_probs(p, i):
                qt = i % 4
                pe.wait_ge(p_ready, 8 * p + i + 1)
                if i >= 2:
                    pe.wait_ge(t_read, 8 * p + i - 1)
                for kb in range(qt + 1):
                    ins = pe.transpose(bank[5 + i % 2][:, kb * P:(kb + 1) * P],
                                       prob[:, i % 2, kb * P:(kb + 1) * P], ident[:, :])
                ins.then_inc(t_full, 1)

            def turn_v(p):
                pe.wait_ge(acc_act, 7 * p + 5)
                for kb in range(TOK):
                    ins = pe.transpose(bank[7][:, kb * P:(kb + 1) * P], vT[:, kb * P:(kb + 1) * P], ident[:, :])
                ins.then_inc(vo_full, 1)

            def attend(p, head):
                pe.wait_ge(t_read, 8 * p + 4 * head + 4)
                pe.wait_ge(vo_read, 3 * p + 1 + head)
                for kb in range(TOK):
                    ks, q = slice(kb * P, kb * P + P), slice(kb * P, SEQ)
                    ins = mm3(bank[7][:, q], v_hi[:, ks], v_lo[:, ks], pT_hi[:, kb, q], pT_lo[:, kb, q],
                              kb == 0, kb == TOK - 1)
                ins.then_inc(vo_full, 1)

            def pair_steps(p, last):
                for j in range(PAIR_UNITS):
                    pe.wait_ge(lo_done, PAIR_UNITS * p + (FIRST_UNITS + j + 1))
                    if j < RING:
                        if isinstance(p, int):
                            pe.wait_ge(*pair_unit_freed(p - 1, j + 6))
                        else:
                            pe.wait_ge(acc_act, 7 * p + (j + 2))
                    else:
                        pe.wait_ge(*pair_unit_freed(p, j - RING))
                    unit(j % RING, bank[j % RING], h_hi, h_lo).then_inc(unit_done, 1)
                    if last and j == 0:
                        pe.wait_ge(ln_dve, 1)
                        pe.wait_ge(t_read, 8 * p)
                        for n, part in enumerate((t1, t2)):
                            for c in range(2):
                                ins = pe.matmul(bank[5][:, :], mean_w[:, :], part[:, c, :], start=(n + c == 0),
                                                stop=(n + c == 2))
                        ins.then_inc(ln_mm, 1)
                    if last and j == 2:
                        pe.wait_ge(ln_dve, 3)
                        for n, part in enumerate((t1, t2)):
                            for c in range(2):
                                ins = pe.matmul(bank[6][:, :], mean_w[:, :], part[:, c, :], start=(n + c == 0),
                                                stop=(n + c == 2))
                        ins.then_inc(ln_mm, 1)
                    if j == 2:
                        pe.wait_ge(acc_dve, 2 * p + 4)
                        scores(p, 0)
                        scores(p, 1)
                    if j == 3:
                        turn_v(p)
                        scores(p, 2)
                        scores(p, 3)
                        if last:
                            pe.wait_ge(ln_dve, 4)
                        turn_probs(p, 0)
                        turn_probs(p, 1)
                    if j == 4:
                        scores(p, 4)
                        scores(p, 5)
                        turn_probs(p, 2)
                        turn_probs(p, 3)
                        if last:
                            pe.wait_ge(vo_read, 3 * p + 1)
                            for t in range(TOK):
                                ins = pe.transpose(bank[7][:, t * P:(t + 1) * P], t3[:, 0, t * P:(t + 1) * P], ident[:, :])
                            ins.then_inc(ln_mm, 1)
                    if j == 5:
                        if last:
                            pe.wait_ge(ln_dve, 5)
                        attend(p, 0)
                        scores(p, 6)
                        scores(p, 7)
                        turn_probs(p, 4)
                        turn_probs(p, 5)
                    if j == 6:
                        turn_probs(p, 6)
                        turn_probs(p, 7)
                        if last:
                            pe.wait_ge(vo_read, 3 * p + 2)
                            pe.wait_ge(ln_dve, 6)
                            for t in range(TOK):
                                ins = pe.transpose(bank[7][:, t * P:(t + 1) * P], t3[:, 1, t * P:(t + 1) * P], ident[:, :])
                            ins.then_inc(ln_mm, 1)
                    if j == 7:
                        if last:
                            pe.wait_ge(ln_dve, 7)
                        attend(p, 1)
                        if last:
                            pe.wait_ge(br_split, 1)
                            pe.wait_ge(pool_w_split, 2)
                            for c in range(2):
                                mm3(bank[5 + c][:, :], pool_w_hi[:, c, :], pool_w_lo[:, c, :], t1[:, c, :],
                                    t2[:, c, :], True, True).then_inc(br_mm, 1)

            with pe.Fori(0, PAIRS - 1) as p:
                pair_steps(p, False)
            pair_steps(PAIRS - 1, True)

            for m in range(KT):
                u = U_MIX + m
                pe.wait_ge(lo_done, u + 1)
                if m == 0:
                    pe.wait_ge(acc_act, 32)
                    pe.wait_ge(vo_read, 12)
                elif m == 1:
                    pe.wait_ge(s_read, 32)
                else:
                    pe.wait_ge(mix_read, m - 1)
                for i, ks in enumerate((range(0, 4), range(4, 6), range(6, 8))):
                    if m == 0 and i == 1:
                        pe.wait_ge(br_ready, 3)
                    for k in ks:
                        ins = mm3(bank[3 * (m % 2) + i][:, :], w_hi[:, u % RING, k * P:(k + 1) * P],
                                  w_lo[:, u % RING, k * P:(k + 1) * P], br_hi[:, k, :], br_lo[:, k, :],
                                  k == ks[0], k == ks[-1])
                ins.then_inc(unit_done, 1)

            def out_tile(half, t, ks):
                dst = bank[(D0, D1)[half][t]]
                for k in ks:
                    if half == 0 and t == 0:
                        pe.wait_ge(m_lo, k + 1)
                    if t == 0 and k % 2 == 0:
                        pe.wait_ge(lo_done, U_OUT + 4 * half + k // 2 + 1)
                    ts = slice(t * P, (t + 1) * P)
                    ins = mm3(dst[:, :], h_hi[:, k, ts], h_lo[:, k, ts], wo_hi[half][:, k, :], wo_lo[half][:, k, :],
                              k == 0, k == KT - 1)
                return ins

            pe.wait_ge(mix_read, KT - 1)
            for t in range(TOK):
                out_tile(0, t, range(0, 6))
            for t in range(TOK):
                out_tile(0, t, range(6, 8)).then_inc(d0_full, 1)
            pe.wait_ge(mix_read, KT)

            def turn_x1(t):
                pe.wait_ge(xn_done, TOK + t + 1)
                for k in range(KT):
                    b = bank[(D0[t], D1[t])[k // 4]]
                    ins = pe.transpose(b[:, k % 4 * P:(k % 4 + 1) * P], xn[:, t % 2, k * P:(k + 1) * P], ident[:, :])
                ins.then_inc(xt2_done, 1)

            out_tile(1, 0, range(KT)).then_inc(d1_full, 1)
            out_tile(1, 1, range(KT)).then_inc(d1_full, 1)
            out_tile(1, 2, range(KT)).then_inc(d1_full, 1)
            turn_x1(0)
            out_tile(1, 3, range(KT)).then_inc(d1_full, 1)
            turn_x1(1)

            def ff_slot(e):
                return in_ring(U_FF + e) % RING

            for n, (cols, ready) in enumerate(((slice(0, 256), 4), (slice(256, 384), 6), (slice(384, 512), 8))):
                if n:
                    turn_x1(n + 1)
                pe.wait_ge(h2_lo, ready)
                for e in range(3):
                    if n == 0:
                        pe.wait_ge(lo_done, U_FF + e + 1)
                    ins = unit(ff_slot(e), bank[FFB[e]], h_hi, h_lo, cols=cols)
                    if n == 2:
                        ins.then_inc(unit_done, 1)

            def ff_unit(j, odd, slot, dst, count):
                pe.wait_ge(lo_done, count)
                if not isinstance(j, int) or j >= 2:
                    pe.wait_ge(u_read if odd else g_read, j - 1)
                unit(slot, bank[dst], h_hi, h_lo).then_inc(unit_done, 1)

            for e in range(3, 8):
                ff_unit(e // 2, e % 2, ff_slot(e), FFB[e % 4], U_FF + e + 1)
            with pe.Fori(0, 3) as i:
                for jj in range(12):
                    ff_unit(i * 6 + (4 + jj // 2), jj % 2, ff_slot(8 + jj), FFB[jj % 4], i * 12 + (U_FF + 8 + jj + 1))

            def down(n, t, k2_):
                half, kp = divmod(n, FF_TILES // 2)
                k, slot, ts = 2 * kp + k2_, in_ring(U_DOWN + n) % RING, slice(t * P, (t + 1) * P)
                ws = slice(k2_ * SEQ, (k2_ + 1) * SEQ)
                return mm3(bank[(Y0, Y1)[half][t]][:, :], f_hi[:, k, ts], f_lo[:, k, ts], w_hi[:, slot, ws],
                           w_lo[:, slot, ws], k == 0, k == FF_TILES - 1)

            for n in range(FF_TILES - 3):
                pe.wait_ge(lo_done, U_DOWN + n + 1)
                if n == 11:
                    pe.wait_ge(u_read, FF_TILES)
                for k2_ in range(2):
                    if n < 11:
                        pe.wait_ge(f_lo_done, 2 * n + k2_ + 1)
                    for t in range(TOK):
                        ins = down(n, t, k2_)
                ins.then_inc(unit_done, 1)
            pe.wait_ge(lo_done, U_END)
            for t in range(TOK):
                for n in range(FF_TILES - 3, FF_TILES):
                    for k2_ in range(2):
                        ins = down(n, t, k2_)
                ins.then_inc(y1_full, 1)


def _raw_count(u, slot):
    return 16 * (u // RING + 1)


D0, D1 = [6, 7, 0, 1], [2, 3, 4, 5]
FFB = [6, 2, 7, 3]
Y0, Y1 = [0, 1, 4, 5], [6, 2, 7, 3]


def bias_onehot():
    one = np.zeros((33, BIAS_LEN), np.float32)
    for j in range(BIAS_LEN):
        n = j - 127
        if n < 0:
            one[32, j] = 1.0
        elif n < 16:
            one[n, j] = 1.0
        else:
            one[min(31, 16 + int(math.log(n / 16) / math.log(8) * 16)), j] = 1.0
    return one


def pooling_constants():
    c = np.zeros((P, C_LEN), np.float32)
    for tile in range(2):
        for half in range(2):
            w = (2, 4, 8, 16)[2 * tile + half]
            rows = slice(64 * half, 64 * half + 64)
            c[rows, 16 * tile:16 * tile + 16] = w / np.minimum(np.arange(1, 17), w)
            c[rows, C_INV + tile] = 1.0 / w
    return c


def kernel(**inputs):
    import numpy as _np
    import concourse.bacc as _bacc
    from concourse import mybir as _mybir
    from concourse.bass_utils import run_bass_kernel_spmd as _run

    a = {k: _np.asarray(v) for k, v in inputs.items()}

    def columns(v):
        return v.reshape(-1, P).T

    vecs = _np.concatenate(
        [columns(a["pre_mix_g"][0]), columns(a["b_gate"][0]), columns(a["pool_scale"][0]), columns(a["b_dw"][0]),
         columns(a["conv_ln_g"][0]), columns(a["conv_ln_b"][0]), a["w_dw"][0].T[:P], a["w_dw"][0].T[P:]], axis=1)
    w_branch = _np.concatenate([a["w_attn_o"][0], a["w_pool_o"][0], a["w_conv_o"][0]], axis=0)
    feeds = [("x", a["x"]), ("w_in", a["w_in"]), ("w_branch", w_branch), ("w_out", a["w_out"]),
             ("w_ffn_in", a["w_ffn_in"]), ("w_ffn_out", a["w_ffn_out"]), ("vecs", vecs),
             ("post_mix_g", a["post_mix_g"]), ("pre_ffn_g", a["pre_ffn_g"]), ("post_ffn_g", a["post_ffn_g"]),
             ("rel_bias", a["rel_bias"]), ("w_pool_g", a["w_pool_g"]), ("onehot", bias_onehot()),
             ("pool_const", pooling_constants())]
    nc = _bacc.Bacc("TRN2", target_bir_lowering=False, num_devices=1)
    arrays, args = {}, []
    for name, value in feeds:
        value = _np.ascontiguousarray(value)
        arrays[f"in_{name}_dram"] = value
        args.append(nc.dram_tensor(f"in_{name}_dram", value.shape, _mybir.dt.from_np(value.dtype),
                                   kind="ExternalInput").ap())
    args.append(nc.dram_tensor("out_0_dram", (1, SEQ, D_MODEL), F32, kind="ExternalOutput").ap())
    build(nc, *args)
    r = _run(nc, [arrays], core_ids=[0])
    return r.results[0]["out_0_dram"]
```

```python
import math
from contextlib import ExitStack

import numpy as np

import concourse.bass as bass
from concourse import mybir

F32 = mybir.dt.float32
F32R = mybir.dt.float32r
BF16 = mybir.dt.bfloat16
ALU = mybir.AluOpType
ACT = mybir.ActivationFunctionType

P = 128
SEQ = 512
D_MODEL = 1024
DFF = 2816
TOK = SEQ // P
KT = D_MODEL // P
PAIRS = 4
HEAD = 64
ATT = 512
GATES = 3 * KT
COL_Q, COL_K, COL_V, COL_POOL = 0, ATT, 2 * ATT, 3 * ATT
COL_CONV = COL_POOL + 256
COL_GATE = COL_CONV + 512
CONV_K = 31
CONV_PAD = 32
POOL_PAD = 16
EPS = 1e-6
BIAS_LEN = 640
MASKED = -1e30

FIRST_UNITS = 6
PAIR_UNITS = 9
U_MIX = FIRST_UNITS + PAIRS * PAIR_UNITS
U_OUT = U_MIX + KT
U_FF = U_OUT + 8
FF_TILES = DFF // P
U_DOWN = U_FF + 2 * FF_TILES
U_END = U_DOWN + FF_TILES
RING = 3

V_PRE, V_GATE, V_PSCALE, V_BDW, V_LNG, V_LNB, V_DW = 0, 8, 32, 34, 36, 38, 40
V_LEN = 40 + 2 * CONV_K
C_RATIO, C_INV = 0, 32
C_LEN = 34
HEAD_ROWS = (slice(0, HEAD), slice(HEAD, P))


def in_ring(u):
    return u if u < U_OUT else u - 8


def build(nc, x, w_in, w_branch, w_out, w_ffn_in, w_ffn_out, vecs, post_mix_g, pre_ffn_g, post_ffn_g,
          rel_bias, w_pool_g, onehot, pool_const, out):
    bias_scratch = nc.dram_tensor("bias_scratch", (2 * PAIRS, BIAS_LEN), F32, kind="Internal").ap()

    base = 16512

    def at(name, kb, shape, dtype=F32):
        return nc.alloc_sbuf_tensor_at(name, [P] + shape, dtype, offset=base + int(kb * 1024))

    raw = at("raw", 0, [RING, 1024])
    w_hi = at("w_hi", 12, [RING, 1024], F32R)
    w_lo = at("w_lo", 24, [RING, 1024], F32R)
    h_hi = at("h_hi", 36, [KT, SEQ], F32R)
    h_lo = at("h_lo", 52, [KT, SEQ], F32R)
    gate = at("gate", 68, [GATES, SEQ])
    br_hi = at("br_hi", 116, [KT, SEQ], F32R)
    br_lo = at("br_lo", 132, [KT, SEQ], F32R)
    onehot_sb = at("onehot_sb", 68, [BIAS_LEN])
    table = at("table", 71, [8])
    bias_vec = at("bias_vec", 72, [BIAS_LEN])
    junk_x = at("junk_x", 76, [D_MODEL], BF16)
    conv_gate = at("conv_gate", 96, [2, SEQ])
    u_pool = at("u_pool", 190, [2, POOL_PAD + SEQ])
    sum_a = at("sum_a", 194.25, [2, POOL_PAD + SEQ])
    sum_b = at("sum_b", 109, [2, POOL_PAD + SEQ])
    u_conv = at("u_conv", 124, [2, CONV_PAD + SEQ])
    d_pool = at("d_pool", 140, [2, SEQ])
    conv_acc = at("conv_acc", 144, [2, SEQ])
    x_tok = at("x_tok", 162, [TOK, D_MODEL])
    q_parts = at("q_parts", 148, [2, SEQ], F32R)
    k_hi2 = at("k_hi2", 152, [2, SEQ], F32R)
    kT_lo = at("kT_lo", 114, [SEQ], F32R)
    vT = at("vT", 156, [SEQ])
    o_sum = at("o_sum", 156, [SEQ])
    v_parts = at("v_parts", 158, [2, TOK, P], F32R)
    pT_hi = at("pT_hi", 162, [TOK, SEQ], F32R)
    pT_lo = at("pT_lo", 170, [TOK, SEQ], F32R)
    neg_logit = at("neg_logit", 178, [2, SEQ])
    prob = at("prob", 182, [2, SEQ])
    bias_h = at("bias_h", 186, [2, SEQ])
    t1 = at("t1", 190, [2, SEQ], F32R)
    t2 = at("t2", 194, [2, SEQ], F32R)
    t3 = at("t3", 198, [2, SEQ])
    mix = at("mix", 190, [2, 3, SEQ])
    wo_hi = [at("wo0_hi", 148, [KT, SEQ], F32R), at("wo1_hi", 68, [KT, SEQ], F32R)]
    wo_lo = [at("wo0_lo", 164, [KT, SEQ], F32R), at("wo1_lo", 84, [KT, SEQ], F32R)]
    x1 = at("x1", 180, [TOK, D_MODEL])
    gain = at("gain", 196, [D_MODEL])
    junk = at("junk", 200, [D_MODEL], BF16)
    xn = at("xn", 100, [2, D_MODEL])
    y_gain = at("y_gain", 108, [D_MODEL])
    gain_ffn = at("gain_ffn", 112, [D_MODEL])
    f_hi = at("f_hi", 68, [FF_TILES, SEQ], F32R)
    f_lo = at("f_lo", 112, [FF_TILES, SEQ], F32R)
    ff_tanh = at("ff_tanh", 156, [2, SEQ])
    ff_silu = at("ff_silu", 160, [2, SEQ])
    ff_prod = at("ff_prod", 164, [2, SEQ])
    yg0 = at("yg0", 36, [TOK, SEQ])
    yg1 = at("yg1", 44, [2, SEQ])
    ident = at("ident", 202, [P])
    mean_w = at("mean_w", 202.5, [P], F32R)
    pool_w = at("pool_w", 203, [2, P])
    pool_w_hi = at("pool_w_hi", 204, [2, P], F32R)
    pool_w_lo = at("pool_w_lo", 205, [2, P], F32R)
    vec = at("vec", 206, [V_LEN])
    const = at("const", 206.5, [C_LEN])
    half_bias = at("half_bias", 206.75, [GATES])
    half_dw = at("half_dw", 207, [2 * CONV_K])
    neg_max = at("neg_max", 207.25, [8])
    row_sum = at("row_sum", 207.28125, [8])
    row_inv = at("row_inv", 207.3125, [8])
    stat = at("stat", 207.34375, [96])
    spare = at("spare", 207.75, [8])

    with ExitStack() as ctx:
        bank = [ctx.enter_context(nc.psum_tensor(f"bank{i}", [P, SEQ], F32)) for i in range(8)]

        def sem(name):
            return ctx.enter_context(nc.semaphore(name))

        raw_full = [sem(f"raw_full{i}") for i in range(RING)]
        x_full = [sem(f"x_full{i}") for i in range(TOK)]
        x1_full = [sem("x1_full0"), sem("x1_full1")]
        gain_full, vec_full, tab_full, pool_w_full = (
            sem("gain_full"), sem("vec_full"), sem("tab_full"), sem("pool_w_full"))
        bias_stored, bias_full, out_stored = sem("bias_stored"), sem("bias_full"), sem("out_stored")
        hi_done, lo_done, unit_done = sem("hi_done"), sem("lo_done"), sem("unit_done")
        ident_done, prep_done, pads_done, pool_w_split = (
            sem("ident_done"), sem("prep_done"), sem("pads_done"), sem("pool_w_split"))
        vec_mm, vec_read = sem("vec_mm"), sem("vec_read")
        sq_done, pool_tick, rstd_done, xn_done, xt_done = (
            sem("sq_done"), sem("pool_tick"), sem("rstd_done"), sem("xn_done"), sem("xt_done"))
        h_hi_done, h_lo_done = sem("h_hi_done"), sem("h_lo_done")
        acc_act, acc_dve, qk_hi = sem("acc_act"), sem("acc_dve"), sem("qk_hi")
        s_full, s_read, exp_done, inv_done, p_ready = (
            sem("s_full"), sem("s_read"), sem("exp_done"), sem("inv_done"), sem("p_ready"))
        t_full, t_hi, t_read = sem("t_full"), sem("t_hi"), sem("t_read")
        vo_full, vo_hi, vo_read = sem("vo_full"), sem("vo_hi"), sem("vo_read")
        o_moved, o_summed = sem("o_moved"), sem("o_summed")
        conv_step, ln_act, ln_dve, ln_mm, ln_rstd, d_done, br_split, br_mm, br_act, br_ready = (
            sem("conv_step"), sem("ln_act"), sem("ln_dve"), sem("ln_mm"), sem("ln_rstd"), sem("d_done"),
            sem("br_split"), sem("br_mm"), sem("br_act"), sem("br_ready"))
        mix_read, mix_part, mix_sum, m_hi, m_lo = sem("mix_read"), sem("mix_part"), sem("mix_sum"), sem("m_hi"), sem("m_lo")
        d0_full, d1_full, yg_done, x1_done, h2_hi, h2_lo, xt2_done = (
            sem("d0_full"), sem("d1_full"), sem("yg_done"), sem("x1_done"), sem("h2_hi"), sem("h2_lo"),
            sem("xt2_done"))
        tanh_done, g_read, u_read, f_hi_done, f_lo_done = (
            sem("tanh_done"), sem("g_read"), sem("u_read"), sem("f_hi_done"), sem("f_lo_done"))
        y1_full, y_gained, out_ready = sem("y1_full"), sem("y_gained"), sem("out_ready")

        block = ctx.enter_context(nc.Block())

        x_tiles = x[0].rearrange("(t p) d -> p t d", p=P)
        w_in_k = w_in[0].rearrange("(k p) n -> p k n", p=P)
        w_br_k = w_branch.rearrange("(k p) n -> p k n", p=P)
        w_out_k = w_out[0].rearrange("(k p) n -> p k n", p=P)
        w_up_k = w_ffn_in[0].rearrange("(k p) n -> p k n", p=P)
        w_dn_k = w_ffn_out[0].rearrange("(k p) n -> p k n", p=P)

        def k8(tile):
            return tile.rearrange("p (k c) -> p k c", k=8)

        def k2(tile):
            return tile.rearrange("p (k c) -> p k c", k=2)

        def pair_unit_freed(p, j):
            if j < 2:
                return acc_dve, 2 + 2 * p + j + 1
            return acc_act, 4 + 7 * p + (j - 2) + 1

        FIRST_FREED = [(acc_act, 1), (acc_dve, 1), (acc_act, 2), (acc_dve, 2), (acc_act, 3), (acc_act, 4)]

        @block.sync
        def _(sp):
            def load(u, slot, src, view):
                if not (isinstance(u, int) and u < RING):
                    sp.wait_ge(lo_done, u - RING + 1)
                sp.dma_start(view(raw[:, slot, :]), src).then_inc(raw_full[slot], 16)

            for t in range(TOK):
                sp.dma_start(x_tok[:, t, :], x[0, t * P:(t + 1) * P, :]).then_inc(x_full[t], 16)
            first = [COL_CONV + 256, COL_CONV, COL_CONV + 384, COL_CONV + 128, COL_POOL, COL_POOL + 128]
            for u, col in enumerate(first):
                load(u, u % RING, w_in_k[:, :, col:col + P], k8)
                if u == 0:
                    sp.dma_start(vec[:, :], vecs).then_inc(vec_full, 16)
                    sp.dma_start(const[:, :], pool_const).then_inc(vec_full, 16)
                if u == 2:
                    sp.dma_start(onehot_sb[0:33, :], onehot).then_inc(tab_full, 16)
                    sp.dma_start(table[0:32, :], rel_bias).then_inc(tab_full, 16)
                    sp.wait_ge(prep_done, 1)
                    for g in range(4):
                        r0, c = (g % 2) * 64, g // 2
                        sp.dma_start(pool_w[r0:r0 + 64, c, r0:r0 + 64], w_pool_g[0, g]).then_inc(pool_w_full, 16)

            def pair_loads(p):
                for j in range(PAIR_UNITS):
                    col = [COL_Q, COL_K, COL_V][j] + P * p if j < 3 else COL_GATE + 6 * P * p + P * (j - 3)
                    load(FIRST_UNITS + PAIR_UNITS * p + j, j % RING, w_in_k[:, :, bass.ds(col, P)], k8)
                    if j == 3:
                        src = bass.AP(bias_scratch.tensor, p * (2 * BIAS_LEN), [[1, P], [BIAS_LEN, 2], [1, SEQ]])
                        sp.dma_start(bias_h[:, :, :], src).then_inc(bias_full, 16)

            sp.wait_ge(bias_stored, 16)
            with sp.Fori(0, PAIRS) as p:
                pair_loads(p)
            for m in range(KT):
                u = U_MIX + m
                load(u, u % RING, w_br_k[:, :, m * P:(m + 1) * P], k8)
                if m == 3:
                    sp.wait_ge(vo_read, 12)
                    sp.dma_start(x1[:, 0:2, :], x_tiles[:, 0:2, :]).then_inc(x1_full[0], 16)
            for n in range(8):
                u = U_OUT + n
                half, kp = n // 4, n % 4
                load(u, u % RING, w_out_k[:, 2 * kp:2 * kp + 2, half * SEQ:(half + 1) * SEQ], k2)
                if n == 7:
                    sp.wait_ge(m_lo, KT)
                    sp.dma_start(gain[:, :], bass.AP(post_mix_g.tensor, 0, [[0, P], [1, D_MODEL]])).then_inc(gain_full, 16)
                    sp.dma_start(gain_ffn[:, :], bass.AP(pre_ffn_g.tensor, 0, [[0, P], [1, D_MODEL]])).then_inc(gain_full, 16)
                    sp.dma_start(x1[:, 2:4, :], x_tiles[:, 2:4, :]).then_inc(x1_full[1], 16)

            def ff_load(e, slot):
                j, odd = divmod(e, 2)
                load(U_FF + e, slot, w_up_k[:, :, odd * DFF + j * P:odd * DFF + (j + 1) * P], k8)

            for e in range(8):
                ff_load(e, (U_FF + e) % RING)
            sp.wait_ge(x1_done, TOK)
            sp.dma_start(gain[:, :], bass.AP(post_ffn_g.tensor, 0, [[0, P], [1, D_MODEL]])).then_inc(gain_full, 16)
            with sp.Fori(0, 3) as i:
                for jj in range(12):
                    col = i * (6 * P) + (jj % 2) * DFF + (4 + jj // 2) * P
                    load(U_FF + 8 + i * 12 + jj, (U_FF + 8 + jj) % RING, w_up_k[:, :, bass.ds(col, P)], k8)
            for n in range(FF_TILES):
                half, kp = divmod(n, FF_TILES // 2)
                u = U_DOWN + n
                load(u, u % RING, w_dn_k[:, 2 * kp:2 * kp + 2, half * SEQ:(half + 1) * SEQ], k2)
            for t in range(TOK):
                for half in range(2):
                    sp.wait_ge(out_ready, 2 * t + half + 1)
                    sp.dma_start(out[0, t * P:(t + 1) * P, half * SEQ:(half + 1) * SEQ],
                                 x1[:, t, half * SEQ:(half + 1) * SEQ]).then_inc(out_stored, 16)
            sp.wait_ge(out_stored, 16 * 2 * TOK)

        @block.gpsimd
        def _(pool):
            pool.memset(ident[:, :], 0.0).then_inc(pool_tick, 1)
            pool.wait_ge(pool_tick, 1)
            pool.affine_select(out=ident[:, :], in_=ident[:, :], compare_op=ALU.not_equal, fill=1.0, base=0,
                               pattern=[[-1, P]], channel_multiplier=1).then_inc(ident_done, 1)
            tick = 1

            def rsqrt(col_in, col_tmp, col_out, mult, eps):
                nonlocal tick
                pool.tensor_scalar(stat[:, col_tmp:col_tmp + 1], stat[:, col_in:col_in + 1], mult, eps,
                                   ALU.mult, ALU.add).then_inc(pool_tick, 1)
                tick += 1
                pool.wait_ge(pool_tick, tick)
                return pool.tensor_tensor(stat[:, col_out:col_out + 1], stat[:, col_tmp:col_tmp + 1],
                                          stat[:, 95:96], ALU.pow)

            pool.memset(stat[:, 88:96], -0.5).then_inc(pool_tick, 1)
            tick += 1
            pool.wait_ge(pool_tick, tick)
            for t in range(TOK):
                pool.wait_ge(sq_done, t + 1)
                rsqrt(t, 4 + t, 8 + t, 1.0 / D_MODEL, EPS).then_inc(rstd_done, 1)

            pool.memset(u_conv[:, :, 0:CONV_PAD], 0.0).then_inc(pads_done, 1)
            pool.memset(u_pool[:, :, 0:POOL_PAD], 0.0).then_inc(pads_done, 1)
            pool.wait_ge(pads_done, 2)
            pool.wait_ge(acc_act, 4)
            n = POOL_PAD + SEQ

            def link(ins):
                nonlocal tick
                ins.then_inc(pool_tick, 1)
                tick += 1
                pool.wait_ge(pool_tick, tick)

            link(pool.tensor_tensor(sum_a[:, :, 1:n], u_pool[:, :, 1:n], u_pool[:, :, 0:n - 1], ALU.add))
            link(pool.tensor_tensor(sum_b[:, :, 3:n], sum_a[:, :, 3:n], sum_a[:, :, 1:n - 2], ALU.add))
            link(pool.tensor_tensor(sum_a[:, 1, 7:n], sum_b[:, 1, 7:n], sum_b[:, 1, 3:n - 4], ALU.add))
            link(pool.tensor_tensor(sum_b[64:P, 1, 15:n], sum_a[64:P, 1, 15:n], sum_a[64:P, 1, 7:n - 8], ALU.add))
            ratio = const[:, C_RATIO:C_RATIO + 32].rearrange("p (c t) -> p c t", c=2)
            for lo, s in ((0, sum_a), (64, sum_b)):
                rows = slice(lo, lo + 64)
                link(pool.tensor_tensor(s[rows, :, POOL_PAD:POOL_PAD + 16], s[rows, :, POOL_PAD:POOL_PAD + 16],
                                        ratio[rows, :, :], ALU.mult))
                for c in range(2):
                    link(pool.tensor_scalar(s[rows, c, POOL_PAD:n], s[rows, c, POOL_PAD:n],
                                            const[rows, C_INV + c:C_INV + c + 1], None, ALU.mult))
                pool.tensor_tensor(d_pool[rows, :, :], s[rows, :, POOL_PAD:n], u_pool[rows, :, POOL_PAD:n],
                                   ALU.subtract).then_inc(d_done, 1)
            pool.wait_ge(ln_dve, 5)
            pool.tensor_tensor(stat[:, 68:72], stat[:, 64:68], stat[:, 88:92], ALU.pow).then_inc(ln_rstd, 1)
            for m in range(KT - 1):
                b = m % 2
                pool.wait_ge(mix_read, m + 1)
                link(pool.tensor_tensor(mix[:, b, 0, :], mix[:, b, 0, :], mix[:, b, 1, :], ALU.add))
                pool.tensor_tensor(mix[:, b, 0, :], mix[:, b, 0, :], mix[:, b, 2, :], ALU.add).then_inc(mix_sum, 1)
            for t in range(TOK):
                pool.wait_ge(sq_done, TOK + 3 * t + 2)
                link(pool.tensor_tensor(stat[:, 24 + t:25 + t], stat[:, 12 + t:13 + t], stat[:, 16 + t:17 + t], ALU.add))
                rsqrt(24 + t, 28 + t, 32 + t, 1.0 / D_MODEL, 4 * EPS).then_inc(rstd_done, 1)
                pool.wait_ge(sq_done, TOK + 3 * t + 3)
                rsqrt(20 + t, 36 + t, 40 + t, 1.0 / D_MODEL, EPS).then_inc(rstd_done, 1)
            pool.wait_ge(sq_done, 16 + TOK)
            link(pool.tensor_scalar(stat[:, 52:56], stat[:, 44:48], 1.0 / D_MODEL, EPS, ALU.mult, ALU.add))
            for t in range(TOK):
                pool.wait_ge(sq_done, 16 + 4 + t + 1)
                link(pool.tensor_scalar(stat[:, 56 + t:57 + t], stat[:, 48 + t:49 + t], 1.0 / D_MODEL,
                                        stat[:, 52 + t:53 + t], ALU.mult, ALU.add))
                pool.tensor_tensor(stat[:, 60 + t:61 + t], stat[:, 56 + t:57 + t], stat[:, 95:96], ALU.pow)\
                    .then_inc(rstd_done, 1)

        @block.scalar
        def _(act):
            def hi(u, slot):
                act.wait_ge(raw_full[slot], _raw_count(u, slot))
                if not (isinstance(u, int) and u < RING):
                    act.wait_ge(unit_done, in_ring(u) - RING + 1 if isinstance(u, int) else u)
                act.activation(w_hi[:, ring_slot(u, slot), :], raw[:, slot, :], ACT.Copy).then_inc(hi_done, 1)

            def ring_slot(u, slot):
                return in_ring(u) % RING

            def hi_at(u, slot, hslot, loads, done):
                act.wait_ge(raw_full[slot], loads)
                act.wait_ge(unit_done, done)
                act.activation(w_hi[:, hslot, :], raw[:, slot, :], ACT.Copy).then_inc(hi_done, 1)

            nsq = 0

            def square_sum(in_, col, scrap):
                nonlocal nsq
                if nsq:
                    act.wait_ge(sq_done, nsq)
                nsq += 1
                act.activation(scrap, in_, ACT.Square, accum_out=stat[:, col:col + 1]).then_inc(sq_done, 1)

            for t in range(TOK):
                act.wait_ge(x_full[t], 16)
                square_sum(x_tok[:, t, :], t, junk_x[:, :])
            hi(0, 0)
            act.wait_ge(vec_full, 32)
            act.wait_ge(xt_done, TOK)
            for k in range(KT):
                act.activation(h_hi[:, k, :], bank[k][:, :], ACT.Copy, scale=vec[:, V_PRE + k:V_PRE + k + 1])\
                   .then_inc(h_hi_done, 1)
            hi(1, 1)
            act.wait_ge(pool_w_full, 64)
            act.activation(pool_w_hi[:, :, :], pool_w[:, :, :], ACT.Copy).then_inc(pool_w_split, 1)

            for u in range(FIRST_UNITS):
                hi(u + 2, (u + 2) % RING)
                if u == 1:
                    act.wait_ge(vec_mm, 1)
                    act.activation(bias_vec[0:8, 0:SEQ], bank[6][0:8, :], ACT.Copy).then_inc(vec_read, 1)
                    act.activation(bias_vec[0:8, SEQ:BIAS_LEN], bank[7][0:8, 0:P], ACT.Copy).then_inc(vec_read, 1)
                    act.wait_ge(vec_read, 2)
                    act.dma_start(bias_scratch, bias_vec[0:8, :]).then_inc(bias_stored, 16)
                if u in (0, 2):
                    act.wait_ge(unit_done, u + 1)
                    act.activation(conv_gate[:, u // 2, :], bank[u % RING][:, :], ACT.Tanh, scale=0.5).then_inc(acc_act, 1)
                if u >= 4:
                    act.wait_ge(unit_done, u + 1)
                    act.activation(u_pool[:, u - 4, POOL_PAD:], bank[u % RING][:, :], ACT.Copy).then_inc(acc_act, 1)

            def exp(p, i):
                w = (i % 4 + 1) * P
                act.wait_ge(s_read, 8 * p + i + 1)
                if i >= 2:
                    act.wait_ge(t_full, 8 * p + i - 1)
                act.activation(prob[:, i % 2, 0:w], neg_logit[:, i % 2, 0:w], ACT.Exp, bias=neg_max[:, i:i + 1],
                               scale=-1.0, accum_out=row_sum[:, i:i + 1]).then_inc(exp_done, 1)

            def pT_hi_part(p, i):
                qt = i % 4
                act.wait_ge(t_full, 8 * p + i + 1)
                if i >= 4:
                    act.wait_ge(vo_full, 3 * p + 2)
                act.activation(pT_hi[:, 0:qt + 1, qt * P:(qt + 1) * P],
                               bank[5 + i % 2][:, 0:(qt + 1) * P].rearrange("p (k c) -> p k c", c=P),
                               ACT.Copy).then_inc(t_hi, 1)

            def v_hi_part(p):
                act.wait_ge(vo_full, 3 * p + 1)
                for head, cols in enumerate(HEAD_ROWS):
                    ins = act.activation(v_parts[:, head, :, cols],
                                         bank[7][:, :].rearrange("p (k c) -> p k c", c=P)[:, :, cols], ACT.Copy)
                ins.then_inc(vo_hi, 1)

            def o_other_part(p, head):
                act.wait_ge(vo_full, 3 * p + 2 + head)
                act.activation(o_sum[HEAD_ROWS[head], :], bank[7][HEAD_ROWS[1 - head], :], ACT.Copy).then_inc(o_moved, 1)

            def o_hi_part(p, head):
                act.wait_ge(o_summed, 2 * p + 1 + head)
                rows = HEAD_ROWS[head]
                act.activation(br_hi[rows, p, :], o_sum[rows, :], ACT.Copy).then_inc(vo_hi, 1)

            def pair_steps(p, last):
                for j in range(PAIR_UNITS):
                    u = FIRST_UNITS + PAIR_UNITS * p + j
                    hi_at(u + 2, (j + 2) % RING, (j + 2) % RING, 16 * (3 * p + 3 + (j + 2) // 3), u)
                    if j == 3:
                        exp(p, 0)
                        exp(p, 1)
                    if j == 4:
                        v_hi_part(p)
                        pT_hi_part(p, 0)
                        pT_hi_part(p, 1)
                        exp(p, 2)
                        exp(p, 3)
                    if j == 5:
                        pT_hi_part(p, 2)
                        pT_hi_part(p, 3)
                        exp(p, 4)
                        exp(p, 5)
                    if j == 6:
                        o_other_part(p, 0)
                        pT_hi_part(p, 4)
                        pT_hi_part(p, 5)
                        o_hi_part(p, 0)
                        exp(p, 6)
                        exp(p, 7)
                    if j == 7:
                        pT_hi_part(p, 6)
                        pT_hi_part(p, 7)
                    if j == 8:
                        o_other_part(p, 1)
                        o_hi_part(p, 1)
                    if last:
                        branch_steps(j)
                    act.wait_ge(unit_done, u + 1)
                    if j == 0:
                        for head, rows in enumerate(HEAD_ROWS):
                            ins = act.activation(q_parts[rows, head, :], bank[j % RING][rows, :], ACT.Copy)
                        ins.then_inc(qk_hi, 1)
                    elif j == 1:
                        for head, rows in enumerate(HEAD_ROWS):
                            for to in HEAD_ROWS:
                                ins = act.activation(k_hi2[to, head, :], bank[j % RING][rows, :], ACT.Copy)
                        ins.then_inc(qk_hi, 1)
                    elif j == 2:
                        act.wait_ge(acc_dve, 2 * p + 3)
                        act.activation(vT[:, :], bank[j % RING][:, :], ACT.Copy).then_inc(acc_act, 1)
                    else:
                        g = 6 * p + (j - 3)
                        act.activation(gate[:, g, :], bank[j % RING][:, :], ACT.Tanh, scale=0.5,
                                       bias=half_bias[:, bass.ds(g, 1)]).then_inc(acc_act, 1)

            def branch_steps(j):
                if j == 0:
                    act.wait_ge(conv_step, 2 * CONV_K)
                    act.wait_ge(d_done, 2)
                    act.activation(t1[:, :, :], conv_acc[:, :, :], ACT.Copy).then_inc(ln_act, 1)
                if j == 1:
                    act.wait_ge(ln_dve, 2)
                    act.activation(t3[:, :, :], conv_acc[:, :, :], ACT.Square).then_inc(ln_act, 1)
                    act.wait_ge(ln_act, 2)
                    act.activation(t1[:, :, :], t3[:, :, :], ACT.Copy).then_inc(ln_act, 1)
                if j == 7:
                    act.wait_ge(ln_dve, 7)
                    for c in range(2):
                        act.activation(conv_acc[:, c, :], conv_acc[:, c, :], ACT.Identity,
                                       scale=vec[:, V_LNG + c:V_LNG + c + 1],
                                       bias=vec[:, V_LNB + c:V_LNB + c + 1]).then_inc(ln_act, 1)
                    act.wait_ge(ln_act, 6)
                    act.activation(t3[:, :, :], conv_acc[:, :, :], ACT.Tanh, scale=0.5).then_inc(ln_act, 1)
                if j == 6:
                    act.activation(t1[:, :, :], d_pool[:, :, :], ACT.Copy).then_inc(ln_act, 1)
                if j == 8:
                    for c in range(2):
                        act.wait_ge(br_mm, c + 1)
                        act.activation(br_hi[:, 4 + c, :], bank[5 + c][:, :], ACT.Copy,
                                       scale=vec[:, V_PSCALE + c:V_PSCALE + c + 1]).then_inc(br_act, 1)
                    act.wait_ge(ln_dve, 9)
                    act.activation(br_hi[:, 6:8, :], t3[:, :, :], ACT.Copy, scale=0.5).then_inc(br_act, 1)

            with act.Fori(0, PAIRS - 1) as p:
                pair_steps(p, False)
            pair_steps(PAIRS - 1, True)

            def merged_hi(m):
                act.wait_ge(mix_sum, m + 1)
                act.activation(h_hi[:, m, :], mix[:, m % 2, 0, :], ACT.Copy).then_inc(m_hi, 1)

            def wo_hi_part(n):
                u = U_OUT + n
                half, kp = divmod(n, 4)
                act.wait_ge(raw_full[u % RING], 16 * (u // RING + 1))
                act.activation(wo_hi[half][:, 2 * kp:2 * kp + 2, :], k2(raw[:, u % RING, :]), ACT.Copy).then_inc(hi_done, 1)

            def hi_int(u):
                hi_at(u, u % RING, in_ring(u) % RING, 16 * (u // RING + 1), in_ring(u) - RING + 1)

            for m in range(KT):
                u = U_MIX + m
                if u + 2 < U_OUT:
                    hi_int(u + 2)
                else:
                    act.wait_ge(vo_full, 12)
                    wo_hi_part(u + 2 - U_OUT)
                if m == KT - 1:
                    wo_hi_part(2)
                    wo_hi_part(3)
                if m:
                    merged_hi(m - 1)
            merged_hi(7)
            act.wait_ge(mix_read, KT)
            for n in range(4, 8):
                wo_hi_part(n)
            act.wait_ge(m_lo, KT)

            def sq_y(t):
                act.wait_ge(d0_full, t + 1)
                square_sum(bank[D0[t]][:, :], 12 + t, junk[:, 0:SEQ])
                act.wait_ge(d1_full, t + 1)
                square_sum(bank[D1[t]][:, :], 16 + t, junk[:, 0:SEQ])

            def sq_x(t):
                act.wait_ge(x1_done, t + 1)
                square_sum(x1[:, t, :], 20 + t, junk[:, :])

            def h2_hi_part(t):
                act.wait_ge(xt2_done, t + 1)
                for q, b in enumerate((D0[t], D1[t])):
                    act.activation(h_hi[:, 4 * q:4 * q + 4, t * P:(t + 1) * P],
                                   bank[b][:, :].rearrange("p (k c) -> p k c", c=P), ACT.Copy).then_inc(h2_hi, 1)

            for t in range(TOK):
                sq_y(t)
                sq_x(t)
                if t < 3:
                    hi_int(U_FF + t)
                if t:
                    h2_hi_part(t - 1)
            h2_hi_part(TOK - 1)

            def f_hi_part(j, b):
                act.wait_ge(u_read, j + 1)
                act.activation(f_hi[:, j, :], ff_prod[:, b, :], ACT.Copy).then_inc(f_hi_done, 1)

            def ff_tanh_part(j, b, g_bank):
                act.wait_ge(unit_done, 2 * j + (in_ring(U_FF) + 1))
                if not isinstance(j, int) or j >= 2:
                    act.wait_ge(g_read, j - 1)
                act.activation(ff_tanh[:, b, :], bank[g_bank][:, :], ACT.Tanh, scale=0.5).then_inc(tanh_done, 1)

            for e in range(8):
                if e >= 1:
                    hi_int(U_FF + 2 + e)
                if e % 2 == 0:
                    j = e // 2
                    if j:
                        f_hi_part(j - 1, (j - 1) % 2)
                    ff_tanh_part(j, j % 2, FFB[e % 4])
            with act.Fori(0, 3) as i:
                for jj in range(12):
                    u0 = U_FF + 10 + jj
                    hi_at(None, u0 % RING, in_ring(u0) % RING, i * 64 + 16 * (u0 // RING + 1),
                          i * 12 + (in_ring(u0) - RING + 1))
                    if jj % 2 == 0:
                        j = i * 6 + (4 + jj // 2)
                        f_hi_part(j - 1, (3 + jj // 2) % 2)
                        ff_tanh_part(j, (jj // 2) % 2, FFB[jj % 4])
            f_hi_part(FF_TILES - 1, 1)
            for n in range(2, FF_TILES):
                hi_int(U_DOWN + n)
                if n == 13:
                    act.wait_ge(unit_done, in_ring(U_DOWN) + 11)
                    for t in range(TOK):
                        square_sum(bank[Y0[t]][:, :], 44 + t, junk[:, 0:SEQ])
            for t in range(TOK):
                act.wait_ge(y1_full, t + 1)
                square_sum(bank[Y1[t]][:, :], 48 + t, junk[:, 0:SEQ])

        @block.vector
        def _(dve):
            def lo(dst, slot, src_hi, count):
                dve.wait_ge(hi_done, count)
                dve.tensor_tensor(dst, src_hi[0], src_hi[1], ALU.subtract).then_inc(lo_done, 1)

            def lo_at(slot, hslot, count):
                lo(w_lo[:, hslot, :], slot, (raw[:, slot, :], w_hi[:, hslot, :].bitcast(F32)), count)

            def lo_int(u):
                lo_at(u % RING, in_ring(u) % RING, u + 1)

            def wo_lo_part(n):
                u = U_OUT + n
                half, kp = divmod(n, 4)
                ks = slice(2 * kp, 2 * kp + 2)
                lo(wo_lo[half][:, ks, :], u % RING, (k2(raw[:, u % RING, :]), wo_hi[half][:, ks, :].bitcast(F32)), u + 1)

            dve.memset(pool_w[:, :, :], 0.0).then_inc(prep_done, 1)
            dve.memset(mean_w[:, :].bitcast(F32), 1.0 / 256).then_inc(prep_done, 1)
            dve.memset(table[32:33, :], 8 * MASKED).then_inc(prep_done, 1)
            for t in range(TOK):
                dve.wait_ge(rstd_done, t + 1)
                dve.tensor_scalar(x_tok[:, t, :], x_tok[:, t, :], stat[:, 8 + t:9 + t], None, ALU.mult).then_inc(xn_done, 1)
            lo_int(0)
            dve.wait_ge(vec_full, 32)
            for k in range(KT):
                dve.wait_ge(h_hi_done, k + 1)
                dve.scalar_tensor_tensor(out=h_lo[:, k, :], in0=bank[k][:, :], scalar=vec[:, V_PRE + k:V_PRE + k + 1],
                                         in1=h_hi[:, k, :].bitcast(F32), op0=ALU.mult, op1=ALU.subtract)\
                   .then_inc(h_lo_done, 1)
            dve.wait_ge(tab_full, 32)
            dve.tensor_scalar(table[0:32, :], table[0:32, :], 8.0, None, ALU.mult).then_inc(prep_done, 1)
            lo_int(1)
            dve.tensor_scalar(half_bias[:, :], vec[:, V_GATE:V_GATE + GATES], 0.5, None, ALU.mult).then_inc(prep_done, 1)
            dve.tensor_scalar(half_dw[:, :], vec[:, V_DW:V_DW + 2 * CONV_K], 0.5, None, ALU.mult).then_inc(prep_done, 1)
            dve.wait_ge(pool_w_split, 1)
            dve.tensor_tensor(pool_w_lo[:, :, :], pool_w[:, :, :], pool_w_hi[:, :, :].bitcast(F32), ALU.subtract)\
               .then_inc(pool_w_split, 1)
            for u in range(FIRST_UNITS):
                lo_int(u + 2)
                if u in (1, 3):
                    c = u // 2
                    dve.wait_ge(unit_done, u + 1)
                    dve.wait_ge(acc_act, c + 1)
                    dve.scalar_tensor_tensor(out=u_conv[:, c, CONV_PAD:], in0=conv_gate[:, c, :], scalar=1.0,
                                             in1=bank[u % RING][:, :], op0=ALU.add, op1=ALU.mult).then_inc(acc_dve, 1)
                if u == 4:
                    dve.wait_ge(acc_dve, 2)
                    dve.wait_ge(prep_done, 6)
                    for c in range(2):
                        w = c * CONV_K + CONV_K - 1
                        dve.tensor_scalar(conv_acc[:, c, :], u_conv[:, c, CONV_PAD:], half_dw[:, w:w + 1],
                                          vec[:, V_BDW + c:V_BDW + c + 1], ALU.mult, ALU.add).then_inc(conv_step, 1)
            dve.wait_ge(pads_done, 2)

            def taps(p, s0):
                for s in (s0, s0 + 1):
                    tap = 10 * p + s
                    for c in range(2):
                        dve.wait_ge(conv_step, 2 * tap + (2 + c - 1))
                        dve.scalar_tensor_tensor(out=conv_acc[:, c, :], in0=u_conv[:, c, bass.ds(tap + 2, SEQ)],
                                                 scalar=half_dw[:, bass.ds(tap + c * CONV_K, 1)],
                                                 in1=conv_acc[:, c, :], op0=ALU.mult, op1=ALU.add).then_inc(conv_step, 1)

            def logits(p, i):
                head, w = i // 4, (i % 4 + 1) * P
                if i == 0:
                    dve.wait_ge(bias_full, 16 * p + 16)
                if i >= 2:
                    dve.wait_ge(exp_done, 8 * p + i - 1)
                dve.wait_ge(s_full, 8 * p + i + 1)
                dve.memset(spare[:, i:i + 1], 0.0)
                dve.tensor_tensor_reduce(neg_logit[:, i % 2, 0:w], bank[3 + i % 2][:, 0:w],
                                         bias_h[:, head, w - 1::-1], -0.125, 3e38, ALU.add, ALU.min,
                                         neg_max[:, i:i + 1]).then_inc(s_read, 1)

            def normalise(p, g):
                dve.wait_ge(exp_done, 8 * p + 2 * g + 2)
                dve.reciprocal(row_inv[:, 2 * g:2 * g + 2], row_sum[:, 2 * g:2 * g + 2]).then_inc(inv_done, 1)
                dve.wait_ge(inv_done, 4 * p + g + 1)
                for i in (2 * g, 2 * g + 1):
                    w = (i % 4 + 1) * P
                    dve.tensor_scalar(prob[:, i % 2, 0:w], prob[:, i % 2, 0:w], row_inv[:, i:i + 1], None, ALU.mult)\
                       .then_inc(p_ready, 1)

            def pT_lo_part(p, i):
                qt = i % 4
                dve.wait_ge(t_hi, 8 * p + i + 1)
                dve.tensor_tensor(pT_lo[:, 0:qt + 1, qt * P:(qt + 1) * P],
                                  bank[5 + i % 2][:, 0:(qt + 1) * P].rearrange("p (k c) -> p k c", c=P),
                                  pT_hi[:, 0:qt + 1, qt * P:(qt + 1) * P].bitcast(F32), ALU.subtract).then_inc(t_read, 1)

            def v_lo_part(p):
                dve.wait_ge(vo_hi, 3 * p + 1)
                for head, cols in enumerate(HEAD_ROWS):
                    ins = dve.tensor_tensor(v_parts[:, head, :, HEAD_ROWS[1 - head]],
                                            bank[7][:, :].rearrange("p (k c) -> p k c", c=P)[:, :, cols],
                                            v_parts[:, head, :, cols].bitcast(F32), ALU.subtract)
                ins.then_inc(vo_read, 1)

            def o_sum_part(p, head):
                dve.wait_ge(o_moved, 2 * p + 1 + head)
                rows = HEAD_ROWS[head]
                dve.tensor_tensor(o_sum[rows, :], bank[7][rows, :], o_sum[rows, :], ALU.add).then_inc(o_summed, 1)

            def o_lo_part(p, head):
                dve.wait_ge(vo_hi, 3 * p + 2 + head)
                rows = HEAD_ROWS[head]
                dve.tensor_tensor(br_lo[rows, p, :], o_sum[rows, :], br_hi[rows, p, :].bitcast(F32), ALU.subtract)\
                   .then_inc(vo_read, 1)

            def pair_steps(p, last):
                for j in range(PAIR_UNITS):
                    lo_at((j + 2) % RING, (j + 2) % RING, PAIR_UNITS * p + (FIRST_UNITS + j + 3))
                    if j == 3:
                        logits(p, 0)
                        logits(p, 1)
                        normalise(p, 0)
                    if j == 4:
                        logits(p, 2)
                        logits(p, 3)
                        v_lo_part(p)
                        pT_lo_part(p, 0)
                        pT_lo_part(p, 1)
                        normalise(p, 1)
                    if j == 5:
                        logits(p, 4)
                        logits(p, 5)
                        pT_lo_part(p, 2)
                        pT_lo_part(p, 3)
                        normalise(p, 2)
                    if j == 6:
                        logits(p, 6)
                        logits(p, 7)
                        o_sum_part(p, 0)
                        pT_lo_part(p, 4)
                        pT_lo_part(p, 5)
                        o_lo_part(p, 0)
                        normalise(p, 3)
                    if j == 7:
                        pT_lo_part(p, 6)
                        pT_lo_part(p, 7)
                    if j == 8:
                        o_sum_part(p, 1)
                        o_lo_part(p, 1)
                    if last:
                        branch_steps(j)
                    elif j in (0, 1, 2, 7, 8):
                        taps(p, {0: 0, 1: 2, 2: 4, 7: 6, 8: 8}[j])
                    if j < 2:
                        dve.wait_ge(qk_hi, 2 * p + j + 1)
                        for head, rows in enumerate(HEAD_ROWS):
                            if j == 0:
                                dst, part = q_parts[HEAD_ROWS[1 - head], head, :], q_parts[rows, head, :]
                            else:
                                dst, part = kT_lo[rows, :], k_hi2[rows, head, :]
                            ins = dve.tensor_tensor(dst, bank[j % RING][rows, :], part.bitcast(F32), ALU.subtract)
                        ins.then_inc(acc_dve, 1)

            def over_tiles(ap):
                return ap.rearrange("p (a t) -> p a t", a=1).to_broadcast([P, 2, SEQ])

            def branch_steps(j):
                if j == 0:
                    dve.wait_ge(ln_act, 1)
                    dve.tensor_tensor(t2[:, :, :], conv_acc[:, :, :], t1[:, :, :].bitcast(F32), ALU.subtract)\
                       .then_inc(ln_dve, 1)
                if j == 1:
                    dve.wait_ge(ln_mm, 1)
                    for c in range(2):
                        ins = dve.tensor_tensor(conv_acc[:, c, :], conv_acc[:, c, :], bank[5][:, :], ALU.subtract)
                    ins.then_inc(ln_dve, 1)
                    dve.wait_ge(ln_act, 3)
                    dve.tensor_tensor(t2[:, :, :], t3[:, :, :], t1[:, :, :].bitcast(F32), ALU.subtract)\
                       .then_inc(ln_dve, 1)
                if j == 3:
                    dve.wait_ge(ln_mm, 2)
                    dve.tensor_scalar(t3[:, 0, :], bank[6][:, :], EPS, None, ALU.add).then_inc(ln_dve, 1)
                if j == 5:
                    dve.wait_ge(ln_mm, 3)
                    dve.tensor_copy(stat[:, 64:68], bank[7][:, 0:SEQ:P]).then_inc(ln_dve, 1)
                    dve.wait_ge(ln_rstd, 1)
                    dve.tensor_copy(t3[:, 1, :].rearrange("p (t c) -> p t c", c=P),
                                    stat[:, 68:72].rearrange("p (t c) -> p t c", c=1).to_broadcast([P, TOK, P]))\
                       .then_inc(ln_dve, 1)
                if j == 6:
                    dve.wait_ge(ln_act, 4)
                    dve.tensor_tensor(t2[:, :, :], d_pool[:, :, :], t1[:, :, :].bitcast(F32), ALU.subtract)\
                       .then_inc(br_split, 1)
                if j == 7:
                    dve.wait_ge(ln_mm, 4)
                    for c in range(2):
                        ins = dve.tensor_tensor(conv_acc[:, c, :], conv_acc[:, c, :], bank[7][:, :], ALU.mult)
                    ins.then_inc(ln_dve, 1)
                if j == 8:
                    dve.wait_ge(ln_act, 7)
                    dve.scalar_tensor_tensor(out=t3[:, :, :], in0=t3[:, :, :], scalar=1.0, in1=conv_acc[:, :, :],
                                             op0=ALU.add, op1=ALU.mult).then_inc(ln_dve, 2)
                if j == 8:
                    for c in range(2):
                        dve.wait_ge(br_act, 1 + c)
                        dve.scalar_tensor_tensor(out=br_lo[:, 4 + c, :], in0=bank[5 + c][:, :],
                                                 scalar=vec[:, V_PSCALE + c:V_PSCALE + c + 1],
                                                 in1=br_hi[:, 4 + c, :].bitcast(F32), op0=ALU.mult,
                                                 op1=ALU.subtract).then_inc(br_ready, 1)
                    dve.wait_ge(br_act, 3)
                    dve.wait_ge(ln_dve, 9)
                    dve.scalar_tensor_tensor(out=br_lo[:, 6:8, :], in0=t3[:, :, :], scalar=0.5,
                                             in1=br_hi[:, 6:8, :].bitcast(F32), op0=ALU.mult, op1=ALU.subtract)\
                       .then_inc(br_ready, 1)

            with dve.Fori(0, PAIRS - 1) as p:
                pair_steps(p, False)
            pair_steps(PAIRS - 1, True)

            def merged_lo(m):
                dve.wait_ge(m_hi, m + 1)
                dve.tensor_tensor(h_lo[:, m, :], mix[:, m % 2, 0, :], h_hi[:, m, :].bitcast(F32), ALU.subtract)\
                   .then_inc(m_lo, 1)

            for m in range(KT):
                u = U_MIX + m
                if u + 2 < U_OUT:
                    lo_int(u + 2)
                else:
                    wo_lo_part(u + 2 - U_OUT)
                if m == KT - 1:
                    wo_lo_part(2)
                dve.wait_ge(unit_done, u + 1)
                if m >= 2:
                    dve.wait_ge(m_lo, m - 1)
                for i in range(3):
                    ins = dve.scalar_tensor_tensor(out=mix[:, m % 2, i, :], in0=gate[:, KT * i + m, :], scalar=1.0,
                                                   in1=bank[MIX_BANK[m % 2] + i][:, :], op0=ALU.add, op1=ALU.mult)
                ins.then_inc(mix_read, 1)
                if m == KT - 1:
                    dve.wait_ge(mix_read, KT)
                    dve.tensor_tensor(mix[:, 1, 0, :], mix[:, 1, 0, :], mix[:, 1, 1, :], ALU.add).then_inc(mix_part, 1)
                    dve.wait_ge(mix_part, 1)
                    dve.wait_ge(mix_sum, KT - 1)
                    dve.tensor_tensor(mix[:, 1, 0, :], mix[:, 1, 0, :], mix[:, 1, 2, :], ALU.add).then_inc(mix_sum, 1)
                if m:
                    merged_lo(m - 1)
            merged_lo(7)
            wo_lo_part(3)
            for n in range(4, 8):
                wo_lo_part(n)

            def residual(t):
                if t == 0:
                    dve.wait_ge(gain_full, 32)
                else:
                    dve.wait_ge(x1_done, t)
                if t % 2 == 0:
                    dve.wait_ge(x1_full[t // 2], 16)
                dve.wait_ge(sq_done, TOK + 3 * t + 1)
                dve.tensor_tensor(y_gain[:, 0:SEQ], bank[D0[t]][:, :], gain[:, 0:SEQ], ALU.mult).then_inc(yg_done, 1)
                dve.wait_ge(sq_done, TOK + 3 * t + 2)
                dve.tensor_tensor(y_gain[:, SEQ:], bank[D1[t]][:, :], gain[:, SEQ:], ALU.mult).then_inc(yg_done, 1)
                dve.wait_ge(yg_done, 2 * t + 2)
                dve.wait_ge(rstd_done, TOK + 2 * t + 1)
                dve.scalar_tensor_tensor(out=x1[:, t, :], in0=y_gain[:, :], scalar=stat[:, 32 + t:33 + t],
                                         in1=x1[:, t, :], op0=ALU.mult, op1=ALU.add).then_inc(x1_done, 1)

            def norm_x1(t):
                dve.wait_ge(rstd_done, TOK + 2 * t + 2)
                if t >= 2:
                    dve.wait_ge(xt2_done, t - 1)
                dve.scalar_tensor_tensor(out=xn[:, t % 2, :], in0=x1[:, t, :], scalar=stat[:, 40 + t:41 + t],
                                         in1=gain_ffn[:, :], op0=ALU.mult, op1=ALU.mult).then_inc(xn_done, 1)

            def h2_lo_part(t):
                for q, b in enumerate((D0[t], D1[t])):
                    dve.wait_ge(h2_hi, 2 * t + q + 1)
                    dve.tensor_tensor(h_lo[:, 4 * q:4 * q + 4, t * P:(t + 1) * P],
                                      bank[b][:, :].rearrange("p (k c) -> p k c", c=P),
                                      h_hi[:, 4 * q:4 * q + 4, t * P:(t + 1) * P].bitcast(F32), ALU.subtract)\
                       .then_inc(h2_lo, 1)

            for t in range(TOK):
                residual(t)
                norm_x1(t)
                if t < 3:
                    lo_int(U_FF + t)
                if t:
                    h2_lo_part(t - 1)
            h2_lo_part(TOK - 1)

            def f_lo_part(j, b):
                dve.wait_ge(f_hi_done, j + 1)
                dve.tensor_tensor(f_lo[:, j, :], ff_prod[:, b, :], f_hi[:, j, :].bitcast(F32), ALU.subtract)\
                   .then_inc(f_lo_done, 1)

            def silu_part(j, b, g_bank):
                dve.wait_ge(tanh_done, j + 1)
                if not isinstance(j, int) or j >= 2:
                    dve.wait_ge(u_read, j - 1)
                dve.scalar_tensor_tensor(out=ff_silu[:, b, :], in0=ff_tanh[:, b, :], scalar=1.0,
                                         in1=bank[g_bank][:, :], op0=ALU.add, op1=ALU.mult).then_inc(g_read, 1)

            def prod_part(j, b, u_bank):
                dve.wait_ge(unit_done, 2 * j + (in_ring(U_FF) + 2))
                dve.wait_ge(g_read, j + 1)
                if not isinstance(j, int) or j >= 2:
                    dve.wait_ge(f_lo_done, j - 1)
                dve.scalar_tensor_tensor(out=ff_prod[:, b, :], in0=ff_silu[:, b, :], scalar=0.5,
                                         in1=bank[u_bank][:, :], op0=ALU.mult, op1=ALU.mult).then_inc(u_read, 1)

            for e in range(8):
                j = e // 2
                if e >= 1:
                    lo_int(U_FF + 2 + e)
                if e % 2 == 0:
                    if j:
                        f_lo_part(j - 1, (j - 1) % 2)
                    silu_part(j, j % 2, FFB[e % 4])
                else:
                    prod_part(j, j % 2, FFB[e % 4])
            with dve.Fori(0, 3) as i:
                for jj in range(12):
                    u0 = U_FF + 10 + jj
                    lo_at(u0 % RING, in_ring(u0) % RING, i * 12 + (u0 + 1))
                    j = i * 6 + (4 + jj // 2)
                    if jj % 2 == 0:
                        f_lo_part(j - 1, (3 + jj // 2) % 2)
                        silu_part(j, (jj // 2) % 2, FFB[jj % 4])
                    else:
                        prod_part(j, (jj // 2) % 2, FFB[jj % 4])
            f_lo_part(FF_TILES - 1, 1)
            for n in range(2, FF_TILES):
                lo_int(U_DOWN + n)
                if n == 13:
                    dve.wait_ge(gain_full, 48)
                    for t in range(TOK):
                        dve.wait_ge(sq_done, 16 + t + 1)
                        dve.tensor_tensor(yg0[:, t, :], bank[Y0[t]][:, :], gain[:, 0:SEQ], ALU.mult).then_inc(y_gained, 1)
            for t in range(TOK):
                dve.wait_ge(sq_done, 20 + t + 1)
                if t >= 2:
                    dve.wait_ge(out_ready, 2 * t - 2)
                dve.tensor_tensor(yg1[:, t % 2, :], bank[Y1[t]][:, :], gain[:, SEQ:], ALU.mult).then_inc(y_gained, 1)
                dve.wait_ge(rstd_done, 12 + t + 1)
                r = stat[:, 60 + t:61 + t]
                dve.wait_ge(y_gained, 4 + t + 1)
                dve.scalar_tensor_tensor(out=x1[:, t, 0:SEQ], in0=yg0[:, t, :], scalar=r, in1=x1[:, t, 0:SEQ],
                                         op0=ALU.mult, op1=ALU.add).then_inc(out_ready, 1)
                dve.scalar_tensor_tensor(out=x1[:, t, SEQ:], in0=yg1[:, t % 2, :], scalar=r, in1=x1[:, t, SEQ:],
                                         op0=ALU.mult, op1=ALU.add).then_inc(out_ready, 1)

        @block.tensor
        def _(pe):
            def mm3(dst, a_hi, a_lo, b_hi, b_lo, start, stop):
                pe.matmul(dst, a_hi, b_hi, start=start, stop=False)
                pe.matmul(dst, a_hi, b_lo, start=False, stop=False)
                return pe.matmul(dst, a_lo, b_hi, start=False, stop=stop)

            def unit(slot, dst, m_hi_, m_lo_, before_k=None, cols=slice(0, SEQ)):
                for k in range(KT):
                    if before_k:
                        before_k(k)
                    ins = mm3(dst[:, cols], w_hi[:, slot, k * P:(k + 1) * P], w_lo[:, slot, k * P:(k + 1) * P],
                              m_hi_[:, k, cols], m_lo_[:, k, cols], k == 0, k == KT - 1)
                return ins

            pe.wait_ge(ident_done, 1)
            for t in range(TOK):
                pe.wait_ge(xn_done, t + 1)
                for k in range(KT):
                    ins = pe.transpose(bank[k][:, t * P:(t + 1) * P], x_tok[:, t, k * P:(k + 1) * P], ident[:, :])
                ins.then_inc(xt_done, 1)
            for u in range(FIRST_UNITS):
                pe.wait_ge(lo_done, u + 1)
                if u >= RING:
                    pe.wait_ge(*FIRST_FREED[u - RING])
                unit(u % RING, bank[u % RING], h_hi, h_lo,
                     before_k=(lambda k: pe.wait_ge(h_lo_done, k + 1)) if u == 0 else None).then_inc(unit_done, 1)
                if u == 0:
                    pe.wait_ge(prep_done, 4)
                    pe.matmul(bank[6][0:8, :], table[0:33, :], onehot_sb[0:33, 0:SEQ], start=True, stop=True)
                    pe.matmul(bank[7][0:8, 0:P], table[0:33, :], onehot_sb[0:33, SEQ:BIAS_LEN], start=True, stop=True)\
                      .then_inc(vec_mm, 1)

            def scores(p, i):
                head, qt = divmod(i, 4)
                w = (qt + 1) * P
                rows, q = slice(HEAD * head, HEAD * head + HEAD), slice(qt * P, qt * P + P)
                if i >= 2:
                    pe.wait_ge(s_read, 8 * p + i - 1)
                pe.matmul(bank[3 + i % 2][:, 0:w], q_parts[:, head, q], k_hi2[:, head, 0:w], start=True, stop=False)
                pe.matmul(bank[3 + i % 2][:, 0:w], q_parts[rows, head, q], kT_lo[rows, 0:w], start=False, stop=True)\
                  .then_inc(s_full, 1)

            def turn_probs(p, i):
                qt = i % 4
                pe.wait_ge(p_ready, 8 * p + i + 1)
                if i >= 2:
                    pe.wait_ge(t_read, 8 * p + i - 1)
                for kb in range(qt + 1):
                    ins = pe.transpose(bank[5 + i % 2][:, kb * P:(kb + 1) * P],
                                       prob[:, i % 2, kb * P:(kb + 1) * P], ident[:, :])
                ins.then_inc(t_full, 1)

            def turn_v(p):
                pe.wait_ge(acc_act, 7 * p + 5)
                for kb in range(TOK):
                    ins = pe.transpose(bank[7][:, kb * P:(kb + 1) * P], vT[:, kb * P:(kb + 1) * P], ident[:, :])
                ins.then_inc(vo_full, 1)

            def attend(p, head):
                pe.wait_ge(t_read, 8 * p + 4 * head + 4)
                pe.wait_ge(vo_read, 3 * p + 1 + head)
                for kb in range(TOK):
                    q = slice(kb * P, SEQ)
                    pe.matmul(bank[7][:, q], v_parts[:, head, kb, :], pT_hi[:, kb, q], start=kb == 0, stop=False)
                    ins = pe.matmul(bank[7][:, q], v_parts[:, head, kb, :], pT_lo[:, kb, q], start=False,
                                    stop=kb == TOK - 1)
                ins.then_inc(vo_full, 1)

            def pair_steps(p, last):
                for j in range(PAIR_UNITS):
                    pe.wait_ge(lo_done, PAIR_UNITS * p + (FIRST_UNITS + j + 1))
                    if j < RING:
                        if isinstance(p, int):
                            pe.wait_ge(*pair_unit_freed(p - 1, j + 6))
                        else:
                            pe.wait_ge(acc_act, 7 * p + (j + 2))
                    else:
                        pe.wait_ge(*pair_unit_freed(p, j - RING))
                    unit(j % RING, bank[j % RING], h_hi, h_lo).then_inc(unit_done, 1)
                    if last and j == 0:
                        pe.wait_ge(ln_dve, 1)
                        pe.wait_ge(t_read, 8 * p)
                        for n, part in enumerate((t1, t2)):
                            for c in range(2):
                                ins = pe.matmul(bank[5][:, :], mean_w[:, :], part[:, c, :], start=(n + c == 0),
                                                stop=(n + c == 2))
                        ins.then_inc(ln_mm, 1)
                    if last and j == 2:
                        pe.wait_ge(ln_dve, 3)
                        for n, part in enumerate((t1, t2)):
                            for c in range(2):
                                ins = pe.matmul(bank[6][:, :], mean_w[:, :], part[:, c, :], start=(n + c == 0),
                                                stop=(n + c == 2))
                        ins.then_inc(ln_mm, 1)
                    if j == 2:
                        pe.wait_ge(acc_dve, 2 * p + 4)
                        scores(p, 0)
                        scores(p, 1)
                    if j == 3:
                        turn_v(p)
                        scores(p, 2)
                        scores(p, 3)
                        if last:
                            pe.wait_ge(ln_dve, 4)
                        turn_probs(p, 0)
                        turn_probs(p, 1)
                    if j == 4:
                        scores(p, 4)
                        scores(p, 5)
                        turn_probs(p, 2)
                        turn_probs(p, 3)
                        if last:
                            pe.wait_ge(vo_read, 3 * p + 1)
                            for t in range(TOK):
                                ins = pe.transpose(bank[7][:, t * P:(t + 1) * P], t3[:, 0, t * P:(t + 1) * P], ident[:, :])
                            ins.then_inc(ln_mm, 1)
                    if j == 5:
                        if last:
                            pe.wait_ge(ln_dve, 5)
                        attend(p, 0)
                        scores(p, 6)
                        scores(p, 7)
                        turn_probs(p, 4)
                        turn_probs(p, 5)
                    if j == 6:
                        turn_probs(p, 6)
                        turn_probs(p, 7)
                        if last:
                            pe.wait_ge(vo_read, 3 * p + 2)
                            pe.wait_ge(ln_dve, 6)
                            for t in range(TOK):
                                ins = pe.transpose(bank[7][:, t * P:(t + 1) * P], t3[:, 1, t * P:(t + 1) * P], ident[:, :])
                            ins.then_inc(ln_mm, 1)
                    if j == 7:
                        if last:
                            pe.wait_ge(ln_dve, 7)
                        attend(p, 1)
                        if last:
                            pe.wait_ge(br_split, 1)
                            pe.wait_ge(pool_w_split, 2)
                            for c in range(2):
                                mm3(bank[5 + c][:, :], pool_w_hi[:, c, :], pool_w_lo[:, c, :], t1[:, c, :],
                                    t2[:, c, :], True, True).then_inc(br_mm, 1)

            with pe.Fori(0, PAIRS - 1) as p:
                pair_steps(p, False)
            pair_steps(PAIRS - 1, True)

            for m in range(KT):
                u = U_MIX + m
                pe.wait_ge(lo_done, u + 1)
                if m == 0:
                    pe.wait_ge(s_read, 32)
                    pe.wait_ge(vo_read, 12)
                elif m == 1:
                    pe.wait_ge(acc_act, 32)
                else:
                    pe.wait_ge(mix_read, m - 1)
                for i, ks in enumerate((range(0, 4), range(4, 6), range(6, 8))):
                    if m == 0 and i:
                        pe.wait_ge(br_ready, 1 + i)
                    for k in ks:
                        ins = mm3(bank[MIX_BANK[m % 2] + i][:, :], w_hi[:, u % RING, k * P:(k + 1) * P],
                                  w_lo[:, u % RING, k * P:(k + 1) * P], br_hi[:, k, :], br_lo[:, k, :],
                                  k == ks[0], k == ks[-1])
                ins.then_inc(unit_done, 1)

            def out_tile(half, t, ks):
                dst = bank[(D0, D1)[half][t]]
                for k in ks:
                    if half == 0 and t == 0:
                        pe.wait_ge(m_lo, k + 1)
                    if t == 0 and k % 2 == 0:
                        pe.wait_ge(lo_done, U_OUT + 4 * half + k // 2 + 1)
                    ts = slice(t * P, (t + 1) * P)
                    ins = mm3(dst[:, :], h_hi[:, k, ts], h_lo[:, k, ts], wo_hi[half][:, k, :], wo_lo[half][:, k, :],
                              k == 0, k == KT - 1)
                return ins

            def turn_x1(t):
                pe.wait_ge(xn_done, TOK + t + 1)
                for k in range(KT):
                    b = bank[(D0[t], D1[t])[k // 4]]
                    ins = pe.transpose(b[:, k % 4 * P:(k % 4 + 1) * P], xn[:, t % 2, k * P:(k + 1) * P], ident[:, :])
                ins.then_inc(xt2_done, 1)

            pe.wait_ge(mix_read, KT - 1)
            out_tile(0, 0, range(0, 6))
            out_tile(0, 1, range(0, 6))
            for t in range(TOK):
                if t != 1:
                    out_tile(0, t, range(6, 8) if t == 0 else range(KT)).then_inc(d0_full, 1)
                if t == 0:
                    out_tile(0, 1, range(6, 8)).then_inc(d0_full, 1)
                    pe.wait_ge(mix_read, KT)
                if t >= 2:
                    turn_x1(t - 2)
                out_tile(1, t, range(KT)).then_inc(d1_full, 1)
            turn_x1(2)

            def ff_slot(e):
                return in_ring(U_FF + e) % RING

            for n, (cols, ready) in enumerate(((slice(0, 256), 4), (slice(256, 512), 8))):
                pe.wait_ge(h2_lo, ready)
                for e in range(3):
                    if n == 0 and e == 2:
                        turn_x1(3)
                    if n == 0:
                        pe.wait_ge(lo_done, U_FF + e + 1)
                    ins = unit(ff_slot(e), bank[FFB[e]], h_hi, h_lo, cols=cols)
                    if n == 1:
                        ins.then_inc(unit_done, 1)

            def ff_unit(j, odd, slot, dst, count):
                pe.wait_ge(lo_done, count)
                if not isinstance(j, int) or j >= 2:
                    pe.wait_ge(u_read if odd else g_read, j - 1)
                unit(slot, bank[dst], h_hi, h_lo).then_inc(unit_done, 1)

            for e in range(3, 8):
                ff_unit(e // 2, e % 2, ff_slot(e), FFB[e % 4], U_FF + e + 1)
            with pe.Fori(0, 3) as i:
                for jj in range(12):
                    ff_unit(i * 6 + (4 + jj // 2), jj % 2, ff_slot(8 + jj), FFB[jj % 4], i * 12 + (U_FF + 8 + jj + 1))

            def down(n, t, k2_):
                half, kp = divmod(n, FF_TILES // 2)
                k, slot, ts = 2 * kp + k2_, in_ring(U_DOWN + n) % RING, slice(t * P, (t + 1) * P)
                ws = slice(k2_ * SEQ, (k2_ + 1) * SEQ)
                return mm3(bank[(Y0, Y1)[half][t]][:, :], f_hi[:, k, ts], f_lo[:, k, ts], w_hi[:, slot, ws],
                           w_lo[:, slot, ws], k == 0, k == FF_TILES - 1)

            for n in range(FF_TILES - 3):
                pe.wait_ge(lo_done, U_DOWN + n + 1)
                if n == 11:
                    pe.wait_ge(u_read, FF_TILES)
                for k2_ in range(2):
                    if n < 11:
                        pe.wait_ge(f_lo_done, 2 * n + k2_ + 1)
                    for t in range(TOK):
                        ins = down(n, t, k2_)
                ins.then_inc(unit_done, 1)
            for t in range(TOK):
                for n in range(FF_TILES - 3, FF_TILES):
                    if t == 0:
                        pe.wait_ge(lo_done, U_DOWN + n + 1)
                    for k2_ in range(2):
                        ins = down(n, t, k2_)
                ins.then_inc(y1_full, 1)


def _raw_count(u, slot):
    return 16 * (u // RING + 1)


MIX_BANK = [3, 0]
D0, D1 = [6, 7, 0, 1], [2, 3, 4, 5]
FFB = [6, 2, 7, 3]
Y0, Y1 = [0, 1, 4, 5], [6, 2, 7, 3]


def bias_onehot():
    one = np.zeros((33, BIAS_LEN), np.float32)
    for j in range(BIAS_LEN):
        n = j - 127
        if n < 0:
            one[32, j] = 1.0
        elif n < 16:
            one[n, j] = 1.0
        else:
            one[min(31, 16 + int(math.log(n / 16) / math.log(8) * 16)), j] = 1.0
    return one


def pooling_constants():
    c = np.zeros((P, C_LEN), np.float32)
    for tile in range(2):
        for half in range(2):
            w = (2, 4, 8, 16)[2 * tile + half]
            rows = slice(64 * half, 64 * half + 64)
            c[rows, 16 * tile:16 * tile + 16] = w / np.minimum(np.arange(1, 17), w)
            c[rows, C_INV + tile] = 1.0 / w
    return c


def kernel(**inputs):
    import numpy as _np
    import concourse.bacc as _bacc
    from concourse import mybir as _mybir
    from concourse.bass_utils import run_bass_kernel_spmd as _run

    a = {k: _np.asarray(v) for k, v in inputs.items()}

    def columns(v):
        return v.reshape(-1, P).T

    vecs = _np.concatenate(
        [columns(a["pre_mix_g"][0]), columns(a["b_gate"][0]), columns(a["pool_scale"][0]), columns(a["b_dw"][0]),
         columns(a["conv_ln_g"][0]), columns(a["conv_ln_b"][0]), a["w_dw"][0].T[:P], a["w_dw"][0].T[P:]], axis=1)
    w_branch = _np.concatenate([a["w_attn_o"][0], a["w_pool_o"][0], a["w_conv_o"][0]], axis=0)
    feeds = [("x", a["x"]), ("w_in", a["w_in"]), ("w_branch", w_branch), ("w_out", a["w_out"]),
             ("w_ffn_in", a["w_ffn_in"]), ("w_ffn_out", a["w_ffn_out"]), ("vecs", vecs),
             ("post_mix_g", a["post_mix_g"]), ("pre_ffn_g", a["pre_ffn_g"]), ("post_ffn_g", a["post_ffn_g"]),
             ("rel_bias", a["rel_bias"]), ("w_pool_g", a["w_pool_g"]), ("onehot", bias_onehot()),
             ("pool_const", pooling_constants())]
    nc = _bacc.Bacc("TRN2", target_bir_lowering=False, num_devices=1)
    arrays, args = {}, []
    for name, value in feeds:
        value = _np.ascontiguousarray(value)
        arrays[f"in_{name}_dram"] = value
        args.append(nc.dram_tensor(f"in_{name}_dram", value.shape, _mybir.dt.from_np(value.dtype),
                                   kind="ExternalInput").ap())
    args.append(nc.dram_tensor("out_0_dram", (1, SEQ, D_MODEL), F32, kind="ExternalOutput").ap())
    build(nc, *args)
    r = _run(nc, [arrays], core_ids=[0])
    return r.results[0]["out_0_dram"]
```
